# Optimizing a Trainium2 kernel written in Bass

```python
import jax, jax.numpy as jnp
from jax import lax
import numpy as np

D_MODEL = 1024
BATCH = 1
SEQ = 256
DEPTH = 2

GRID_W = 64
N_FOURIER_GROUPS = 4
FOURIER_GROUP_DIM = D_MODEL // 8
FOURIER_WIDTH = N_FOURIER_GROUPS * FOURIER_GROUP_DIM
CHUNK = 128
N_GATE_GROUPS = 4
GATE_GROUP_DIM = D_MODEL // 8
GATE_WIDTH = N_GATE_GROUPS * GATE_GROUP_DIM
AB_IN_WIDTH = FOURIER_WIDTH + 2 * GATE_WIDTH
AB_OUT_WIDTH = FOURIER_WIDTH + GATE_WIDTH
HEAD_DIM = 128
N_HEADS = D_MODEL // HEAD_DIM
N_KV_HEADS = 2
KV_GROUP = N_HEADS // N_KV_HEADS
QKV_WIDTH = (N_HEADS + 2 * N_KV_HEADS) * HEAD_DIM
Q_BLOCK = 128
ROPE_THETA = 10000.0
ROPE_FREQS_PER_AXIS = HEAD_DIM // 4
D_FF = ((8 * D_MODEL // 3 + 255) // 256) * 256
EPS = 1e-6
N_EVEN = (DEPTH + 1) // 2
N_ODD = DEPTH // 2

kernel_name = "hybrid_fourier_gmlp_axial_gqa_macaron_encoder"

def rmsnorm(x, g):
    xf = x.astype(jnp.float32)
    y = xf * lax.rsqrt(jnp.mean(xf * xf, axis=-1, keepdims=True) + EPS)
    return (y * g.astype(jnp.float32)).astype(x.dtype)

def swiglu(h, w_gate, w_up, w_down):
    return (jax.nn.silu(h @ w_gate) * (h @ w_up)) @ w_down

def fourier_gating_mixer(h, w_in, v_norm, w_s, b_s, w_out):
    B, S, _ = h.shape
    z = h @ w_in
    f = z[..., :FOURIER_WIDTH].reshape(B, S, N_FOURIER_GROUPS, FOURIER_GROUP_DIM)
    f = jnp.fft.fft2(f.astype(jnp.float32), axes=(1, 3), norm="ortho").real
    f = f.astype(h.dtype).reshape(B, S, FOURIER_WIDTH)
    uv = jax.nn.gelu(z[..., FOURIER_WIDTH:])
    u = uv[..., :GATE_WIDTH]
    v = rmsnorm(uv[..., GATE_WIDTH:].reshape(B, S, N_GATE_GROUPS, GATE_GROUP_DIM), v_norm)
    vc = v.reshape(B, S // CHUNK, CHUNK, N_GATE_GROUPS, GATE_GROUP_DIM)
    s = jnp.einsum('gpq,bcqgd->bcpgd', w_s, vc) + b_s.T[None, None, :, :, None]
    gated = u * s.reshape(B, S, GATE_WIDTH)
    return jnp.concatenate([f, gated], axis=-1) @ w_out

def axial_rope_tables(S):
    rows = S // GRID_W
    row_idx = jnp.broadcast_to(jnp.arange(rows)[:, None], (rows, GRID_W)).reshape(S)
    col_idx = jnp.broadcast_to(jnp.arange(GRID_W)[None, :], (rows, GRID_W)).reshape(S)
    inv_freq = ROPE_THETA ** (-jnp.arange(ROPE_FREQS_PER_AXIS, dtype=jnp.float32) / ROPE_FREQS_PER_AXIS)
    ang = jnp.concatenate([row_idx.astype(jnp.float32)[:, None] * inv_freq[None, :],
                           col_idx.astype(jnp.float32)[:, None] * inv_freq[None, :]], axis=-1)
    return jnp.cos(ang), jnp.sin(ang)

def apply_rope(x, cos, sin):
    B, S, H, D = x.shape
    xp = x.astype(jnp.float32).reshape(B, S, H, D // 2, 2)
    x0, x1 = xp[..., 0], xp[..., 1]
    c = cos[None, :, None, :]
    s = sin[None, :, None, :]
    y = jnp.stack([x0 * c - x1 * s, x0 * s + x1 * c], axis=-1)
    return y.reshape(B, S, H, D).astype(x.dtype)

def axial_gqa(h, w_qkv, q_norm, k_norm, w_o):
    B, S, _ = h.shape
    qkv = h @ w_qkv
    q = qkv[..., :N_HEADS * HEAD_DIM].reshape(B, S, N_HEADS, HEAD_DIM)
    k = qkv[..., N_HEADS * HEAD_DIM:(N_HEADS + N_KV_HEADS) * HEAD_DIM].reshape(B, S, N_KV_HEADS, HEAD_DIM)
    v = qkv[..., (N_HEADS + N_KV_HEADS) * HEAD_DIM:].reshape(B, S, N_KV_HEADS, HEAD_DIM)
    cos, sin = axial_rope_tables(S)
    q = apply_rope(rmsnorm(q, q_norm), cos, sin) * (HEAD_DIM ** -0.5)
    k = apply_rope(rmsnorm(k, k_norm), cos, sin)
    nb = S // Q_BLOCK
    qb = q.reshape(B, nb, Q_BLOCK, N_KV_HEADS, KV_GROUP, HEAD_DIM).transpose(1, 0, 2, 3, 4, 5)

    def block(q_blk):
        sc = jnp.einsum('bqkgd,bskd->bkgqs', q_blk, k, preferred_element_type=jnp.float32)
        p = jax.nn.softmax(sc, axis=-1)
        return jnp.einsum('bkgqs,bskd->bqkgd', p.astype(v.dtype), v)

    o = lax.map(block, qb)
    o = o.transpose(1, 0, 2, 3, 4, 5).reshape(B, S, N_HEADS * HEAD_DIM)
    return o @ w_o

def setup_inputs(seed: int = 0) -> dict:
    key = jax.random.key(seed)
    ks = jax.random.split(key, 24)
    f32 = jnp.float32

    def w(k, shape, fan_in):
        return jax.random.normal(k, shape, f32) * (fan_in ** -0.5)

    def gain(k, shape):
        return 1.0 + 0.02 * jax.random.normal(k, shape, f32)

    return {
        "x": jax.random.normal(ks[0], (BATCH, SEQ, D_MODEL), f32),
        "ffn1_norm": gain(ks[1], (DEPTH, D_MODEL)),
        "ffn1_w_gate": w(ks[2], (DEPTH, D_MODEL, D_FF), D_MODEL),
        "ffn1_w_up": w(ks[3], (DEPTH, D_MODEL, D_FF), D_MODEL),
        "ffn1_w_down": w(ks[4], (DEPTH, D_FF, D_MODEL), D_FF),
        "mix_norm": gain(ks[5], (DEPTH, D_MODEL)),
        "ab_w_in": w(ks[6], (N_EVEN, D_MODEL, AB_IN_WIDTH), D_MODEL),
        "ab_v_norm": gain(ks[7], (N_EVEN, N_GATE_GROUPS, GATE_GROUP_DIM)),
        "ab_w_s": w(ks[8], (N_EVEN, N_GATE_GROUPS, CHUNK, CHUNK), CHUNK),
        "ab_b_s": gain(ks[9], (N_EVEN, N_GATE_GROUPS, CHUNK)),
        "ab_w_out": w(ks[10], (N_EVEN, AB_OUT_WIDTH, D_MODEL), AB_OUT_WIDTH),
        "attn_w_qkv": w(ks[11], (N_ODD, D_MODEL, QKV_WIDTH), D_MODEL),
        "attn_q_norm": gain(ks[12], (N_ODD, HEAD_DIM)),
        "attn_k_norm": gain(ks[13], (N_ODD, HEAD_DIM)),
        "attn_w_o": w(ks[14], (N_ODD, N_HEADS * HEAD_DIM, D_MODEL), N_HEADS * HEAD_DIM),
        "ffn2_norm": gain(ks[15], (DEPTH, D_MODEL)),
        "ffn2_w_gate": w(ks[16], (DEPTH, D_MODEL, D_FF), D_MODEL),
        "ffn2_w_up": w(ks[17], (DEPTH, D_MODEL, D_FF), D_MODEL),
        "ffn2_w_down": w(ks[18], (DEPTH, D_FF, D_MODEL), D_FF),
        "final_norm": gain(ks[19], (D_MODEL,)),
    }

def reference(x, ffn1_norm, ffn1_w_gate, ffn1_w_up, ffn1_w_down, mix_norm,
              ab_w_in, ab_v_norm, ab_w_s, ab_b_s, ab_w_out,
              attn_w_qkv, attn_q_norm, attn_k_norm, attn_w_o,
              ffn2_norm, ffn2_w_gate, ffn2_w_up, ffn2_w_down, final_norm):
    for layer in range(DEPTH):
        x = x + 0.5 * swiglu(rmsnorm(x, ffn1_norm[layer]), ffn1_w_gate[layer],
                             ffn1_w_up[layer], ffn1_w_down[layer])
        h = rmsnorm(x, mix_norm[layer])
        i = layer // 2
        if layer % 2 == 0:
            x = x + fourier_gating_mixer(h, ab_w_in[i], ab_v_norm[i], ab_w_s[i],
                                         ab_b_s[i], ab_w_out[i])
        else:
            x = x + axial_gqa(h, attn_w_qkv[i], attn_q_norm[i], attn_k_norm[i], attn_w_o[i])
        x = x + 0.5 * swiglu(rmsnorm(x, ffn2_norm[layer]), ffn2_w_gate[layer],
                             ffn2_w_up[layer], ffn2_w_down[layer])
    return rmsnorm(x, final_norm)


_drawn_inputs = setup_inputs


def setup_inputs(seed=0):
    import zlib

    import numpy as np

    out = dict(_drawn_inputs(seed))
    spreads = {}
    factors = {'ffn1_norm': 4.815,
     'mix_norm': 3.323,
     'ab_v_norm': 7.763,
     'ab_b_s': 7.877,
     'attn_q_norm': 29.54,
     'attn_k_norm': 25.717,
     'ffn2_norm': 6.114,
     'final_norm': 8.028}
    for name, (base, spread) in spreads.items():
        noise = np.random.default_rng([zlib.crc32(name.encode()), seed]).standard_normal(out[name].shape)
        drawn = base * np.exp(spread * noise) if base else spread * noise
        out[name] = __import__('jax').numpy.asarray(drawn.astype(out[name].dtype))
    for name, factor in factors.items():
        out[name] = (out[name] * factor).astype(out[name].dtype)
    return out
```

```python
from contextlib import ExitStack

import numpy as np

import concourse.bass as bass
from concourse import mybir

F32 = mybir.dt.float32
F32R = mybir.dt.float32r
ALU = mybir.AluOpType
ACT = mybir.ActivationFunctionType
AX_X = mybir.AxisListType.X

P = 128
D_MODEL = 1024
SEQ = 256
D_FF = 2816
HEAD_DIM = 128
N_HEADS = 8
N_KV = 2
GRID_W = 64
EPS = 1e-6

KC = D_MODEL // P
FC = D_FF // P
TT = SEQ // P
N_GROUPS = 4

SLOTS = 4
TILES_IN = KC
TILES_OUT = FC // 2
UNIT_MAX = TILES_OUT * P
MIXER_FLOATS = 9744

FFN, MIX, ATT = "ffn", "mix", "att"
PHASES = [FFN, MIX, FFN, FFN, ATT, FFN]
IN_UNITS = {FFN: 2 * FC, MIX: 12, ATT: 12}
OUT_UNITS = {FFN: 2 * KC, MIX: KC, ATT: KC}


def before(counts, n):
    return sum(counts[k] for k in PHASES[:n])


UNIT0 = [before({k: IN_UNITS[k] + OUT_UNITS[k] for k in IN_UNITS}, n) for n in range(len(PHASES))]
PROJ0 = [before(IN_UNITS, n) for n in range(len(PHASES))]
FFN_AT = {n: PHASES[:n].count(FFN) for n in range(len(PHASES)) if PHASES[n] == FFN}
N_NORMS = len(PHASES) + 1
SUMSQ_STEPS = 2 * KC - 1

HEADS = N_KV + N_HEADS
HEAD_UNIT = list(range(N_KV)) + list(range(4, 4 + N_HEADS))
ATT_HEAD_STEPS = [[], [], [("scale", 0), ("scale", 1)], [("norm", 0), ("norm", 1)],
                  [("scale", 2), ("turn", 0), ("turn", 1)], [("scale", 3), ("norm", 2)]]
ATT_HEAD_STEPS += [[("scale", _s - 2), ("norm", _s - 3), ("turn", _s - 4)] for _s in range(6, 12)]
ATT_HEAD_STEPS += [[("norm", HEADS - 1), ("turn", HEADS - 2)], [("turn", HEADS - 1)]]

GATES_AT = {9: (0, 1), 10: (2,), 11: (3,)}

SMALL = []
for _n, _kind in enumerate(PHASES):
    SMALL.append(("rms", _n))
    if _kind == MIX:
        SMALL += [("rcol", _n), ("dft_ch", 0)]
        for _g in range(1, N_GROUPS):
            SMALL += [("dft_pos", _g - 1), ("dft_ch", _g)]
        SMALL += [("dft_pos", N_GROUPS - 1)] + [("spatial", _g) for _g in range(N_GROUPS)]
    if _kind == ATT:
        SMALL += [("rcol", _n)] + [use for uses in ATT_HEAD_STEPS for use in uses if use[0] != "scale"]
SMALL.append(("rms", len(PHASES)))
SMALL_AT = {use: i for i, use in enumerate(SMALL)}

GAIN_V, GAIN_Q, GAIN_K = 0, N_GROUPS, N_GROUPS + 1
N_HEAD_GAINS = N_GROUPS + 2
N_TABLES = 7


def trunk_program(nc, x_t, ffn_in_w, ffn_out_w, mix_w, attn_w, gains, head_gains, spatial_w,
                  spatial_b, dft_channels, dft_positions, rope, matrices, out):
    with ExitStack() as ctx:
        def sb(name, shape, dt=F32):
            return ctx.enter_context(nc.sbuf_tensor(name, shape, dt))

        def sem(name):
            return ctx.enter_context(nc.semaphore(name))

        raw = [sb(f"raw{s}", [P, UNIT_MAX]) for s in range(SLOTS)]
        w_hi = [sb(f"w_hi{s}", [P, UNIT_MAX], F32R) for s in range(SLOTS)]
        w_lo = [sb(f"w_lo{s}", [P, UNIT_MAX], F32R) for s in range(SLOTS)]
        x = sb("x", [P, KC, SEQ])
        xg_hi = sb("xg_hi", [P, KC, SEQ], F32R)
        xg_lo = sb("xg_lo", [P, KC, SEQ], F32R)
        h_hi = sb("h_hi", [P, FC, SEQ], F32R)
        h_lo = sb("h_lo", [P, FC, SEQ], F32R)
        square = sb("square", [P, SEQ])
        sumsq = sb("sumsq", [P, SEQ])
        mean_sq = sb("mean_sq", [P, SEQ])
        rms = sb("rms", [P, SEQ])
        rinv = sb("rinv", [P, SEQ])
        rcol = sb("rcol", [P, TT])
        gate_in = sb("gate_in", [P, SEQ])
        gate_act = sb("gate_act", [P, SEQ])
        up_in = sb("up_in", [P, SEQ])
        inner = sb("inner", [P, SEQ])
        mixers = sb("mixers", [P, MIXER_FLOATS])

        def carve():
            at = [0]

            def part(*dims):
                start, at[0] = at[0], at[0] + int(np.prod(dims))
                flat = mixers[:, start:at[0]]
                if len(dims) == 1:
                    return flat
                if len(dims) == 2:
                    return flat.rearrange("p (a b) -> p a b", a=dims[0])
                return flat.rearrange("p (a b c) -> p a b c", a=dims[0], b=dims[1])
            return part

        part = carve()
        v_in = part(TT, 2, SEQ)
        v_act = part(TT, N_GROUPS * P)
        v_ss = part(TT * N_GROUPS)
        v_ms = part(TT * N_GROUPS)
        v_rms = part(TT * N_GROUPS)
        v_rinv = part(TT * N_GROUPS)
        v_norm = part(TT, N_GROUPS * P)
        f_in = part(2, SEQ)
        f_ch = part(2, TT * 2 * P)
        u_in = part(2, SEQ)
        u_act = part(2, SEQ)
        s_gate = part(SEQ)
        gated = part(SEQ)
        part = carve()
        head_in = part(3, SEQ)
        head_sq = part(2, SEQ)
        head_ms = part(SEQ)
        head_rms = part(SEQ)
        head_rinv = part(SEQ)
        head_n = part(3, SEQ)
        head_cos = part(2, SEQ)
        head_sin = part(SEQ)
        head_t = part(N_KV + N_HEADS, SEQ)
        v_keys = part(TT, N_KV * HEAD_DIM)
        s_max = part(2, TT)
        s_neg = part(2, TT)
        p_sum = part(2, TT)
        p_inv = part(2, TT)
        probs = part(2, TT, SEQ)
        probs_n = part(2, TT, SEQ)
        probs_t = part(2, TT, SEQ)
        gain = sb("gain", [P, N_NORMS, KC])
        head_gain = sb("head_gain", [P, N_HEAD_GAINS])
        w_s = sb("w_s", [P, N_GROUPS, P])
        b_s = sb("b_s", [P, N_GROUPS, TT, P])
        dft_c = sb("dft_c", [P, 2 * P])
        dft_p = sb("dft_p", [P, TT, 2, SEQ])
        cos_sin = sb("cos_sin", [P, 2, SEQ])
        ones = sb("ones", [P, P])
        mats = sb("mats", [P, 2, P])
        ident, swap = mats[:, 0, :], mats[:, 1, :]

        proj = [ctx.enter_context(nc.psum_tensor(f"proj{i}", [P, 512], F32)) for i in range(4)]
        down = [ctx.enter_context(nc.psum_tensor(f"down{i}", [P, 512], F32)) for i in range(2)]
        small = [ctx.enter_context(nc.psum_tensor(f"small{i}", [P, 512], F32)) for i in range(2)]

        raw_landed = [sem(f"raw_landed{s}") for s in range(SLOTS)]
        hi_ready = sem("hi_ready")
        lo_ready = sem("lo_ready")
        unit_done = sem("unit_done")
        proj_read = sem("proj_read")
        small_done = sem("small_done")
        small_read = sem("small_read")
        x_loaded = [sem(f"x_loaded{i}") for i in range(2)]
        gains_loaded = sem("gains_loaded")
        tables_loaded = sem("tables_loaded")
        x_ready = sem("x_ready")
        xg_hi_ready = sem("xg_hi_ready")
        xg_ready = sem("xg_ready")
        sumsq_step = sem("sumsq_step")
        rms_ready = sem("rms_ready")
        gate_ready = sem("gate_ready")
        inner_ready = sem("inner_ready")
        h_hi_ready = sem("h_hi_ready")
        h_ready = sem("h_ready")
        dve_step = sem("dve_step")
        ones_ready = sem("ones_ready")
        rinv_ready = sem("rinv_ready")
        v_act_ready = sem("v_act_ready")
        v_ss_ready = sem("v_ss_ready")
        v_ms_ready = sem("v_ms_ready")
        v_rms_ready = sem("v_rms_ready")
        v_norm_ready = sem("v_norm_ready")
        u_act_ready = sem("u_act_ready")
        gated_ready = sem("gated_ready")
        head_sq_ready = sem("head_sq_ready")
        head_rms_ready = sem("head_rms_ready")
        head_n_ready = sem("head_n_ready")
        head_cos_ready = sem("head_cos_ready")
        head_t_ready = sem("head_t_ready")
        scores_done = sem("scores_done")
        max_ready = sem("max_ready")
        probs_ready = sem("probs_ready")
        probs_n_ready = sem("probs_n_ready")
        turned = sem("turned")
        probs_t_ready = sem("probs_t_ready")
        ctx_done = sem("ctx_done")
        y_ready = sem("y_ready")
        out_written = sem("out_written")

        block = ctx.enter_context(nc.Block())

        def unit(slot, tiles):
            return raw[slot][:, 0:tiles * P], w_hi[slot][:, 0:tiles * P], w_lo[slot][:, 0:tiles * P]

        def h_hi0(n):
            return before({FFN: FC, MIX: KC, ATT: KC}, n)

        def h0(n):
            return before({FFN: FC, MIX: KC - N_GROUPS, ATT: KC}, n)

        @block.sync
        def _(sp):
            def load(slot, source, tiles, splits):
                if splits is not None:
                    sp.wait_ge(lo_ready, splits)
                sp.dma_start(raw[slot][:, 0:tiles * P], source).then_inc(raw_landed[slot], 16)

            tables = ((mats, matrices), (head_gain, head_gains), (w_s, spatial_w), (b_s, spatial_b),
                      (dft_c, dft_channels), (dft_p, dft_positions), (cos_sin, rope))
            assert len(tables) == N_TABLES
            for n, kind in enumerate(PHASES):
                if n == 1:
                    for target, table in tables:
                        sp.dma_start(target[:], table).then_inc(tables_loaded, 16)
                source = {FFN: ffn_in_w, MIX: mix_w, ATT: attn_w}[kind]
                row0 = IN_UNITS[FFN] * FFN_AT[n] if kind == FFN else 0
                count = IN_UNITS[kind] + (OUT_UNITS[kind] if kind != FFN else 0)
                first = 0
                if n == 0:
                    for s in range(SLOTS):
                        load(s, source[s], TILES_IN, None)
                    first = SLOTS
                with sp.Fori(first, count - SLOTS + 1, SLOTS) as u:
                    for s in range(SLOTS):
                        load(s, source[bass.ds(u + row0 + s, 1), :, :].rearrange("u p n -> p (u n)"),
                             TILES_IN, u + UNIT0[n] + s - SLOTS + 1)
                if kind == FFN:
                    with sp.Fori(0, OUT_UNITS[FFN] - SLOTS + 1, SLOTS) as u:
                        for s in range(SLOTS):
                            row = u + OUT_UNITS[FFN] * FFN_AT[n] + s
                            load(s, ffn_out_w[bass.ds(row, 1), :, :].rearrange("u p n -> p (u n)"),
                                 TILES_OUT, u + UNIT0[n] + IN_UNITS[FFN] + s - SLOTS + 1)
            for j in range(KC):
                sp.wait_ge(y_ready, j + 1)
                sp.dma_start(out[:, j, :], head_t[:, j, :]).then_inc(out_written, 16)
            sp.wait_ge(out_written, 16 * KC)

        @block.gpsimd
        def _(pool):
            def sum_squares(n):
                at = SUMSQ_STEPS * n
                for k in range(KC):
                    if n:
                        pool.wait_ge(x_ready, KC * (n - 1) + k + 1)
                    elif k % 4 == 0:
                        pool.wait_ge(x_loaded[k // 4], 16)
                    if k == 0:
                        nc.gpsimd.tensor_tensor(sumsq[:], x[:, 0, :], x[:, 0, :], ALU.mult).then_inc(sumsq_step, 1)
                        at += 1
                        continue
                    pool.wait_ge(sumsq_step, at)
                    nc.gpsimd.tensor_tensor(square[:], x[:, k, :], x[:, k, :], ALU.mult).then_inc(sumsq_step, 1)
                    at += 1
                    pool.wait_ge(sumsq_step, at)
                    nc.gpsimd.tensor_tensor(sumsq[:], sumsq[:], square[:], ALU.add).then_inc(sumsq_step, 1)
                    at += 1

            nc.gpsimd.memset(ones[:], 1.0).then_inc(ones_ready, 1)
            for n in range(N_NORMS):
                sum_squares(n)
                if n < len(PHASES) and PHASES[n] == ATT:
                    for h in range(N_KV + N_HEADS):
                        pool.wait_ge(head_n_ready, h + 1)
                        if h >= 2:
                            pool.wait_ge(head_t_ready, h - 1)
                        nc.gpsimd.tensor_tensor(head_cos[:, h % 2, :], head_n[:, h % 3, :], cos_sin[:, 0, :],
                                                ALU.mult).then_inc(head_cos_ready, 1)

        @block.scalar
        def _(act):
            for half in range(2):
                act.dma_start(x[:, 4 * half:4 * half + 4, :], x_t[:, 4 * half:4 * half + 4, :]).then_inc(x_loaded[half], 16)
                if half == 0:
                    act.dma_start(gain[:], gains).then_inc(gains_loaded, 16)
            def split_hi(u, slot, tiles, landings):
                source, hi, _ = unit(slot, tiles)
                act.wait_ge(raw_landed[slot], landings)
                if u is not None:
                    act.wait_ge(unit_done, u)
                nc.scalar.activation(hi, source, ACT.Copy).then_inc(hi_ready, 1)

            def split_hi_at(u, tiles):
                split_hi(u - SLOTS + 1 if u >= SLOTS else None, u % SLOTS, tiles, 16 * (u // SLOTS + 1))

            def gained(n, k, wait):
                act.wait_ge(*wait)
                nc.scalar.activation(xg_hi[:, k, :], x[:, k, :], ACT.Copy,
                                     scale=gain[:, n, k:k + 1]).then_inc(xg_hi_ready, 1)

            def root(n):
                act.wait_ge(small_read, SMALL_AT[("rms", n)] + 1)
                nc.scalar.activation(rms[:], mean_sq[:], ACT.Sqrt).then_inc(rms_ready, 1)

            def ffn(n):
                u0 = UNIT0[n]

                def chunk(done, slot, landings, c, at, tiles):
                    split_hi(done + 1, slot, tiles, landings)
                    act.wait_ge(proj_read, 2 * c + PROJ0[n] + 1)
                    nc.scalar.activation(gate_act[:], gate_in[:], ACT.Silu).then_inc(gate_ready, 1)
                    act.wait_ge(inner_ready, c + FFN_AT[n] * FC + 1)
                    nc.scalar.activation(at, inner[:], ACT.Copy).then_inc(h_hi_ready, 1)
                    split_hi(done + 2, slot + 1, tiles, landings)

                root(n)
                with act.Fori(0, FC - 2, 2) as c:
                    for k in range(2):
                        chunk(c * 2 + (u0 + 2 * k), 2 * k, c * 8 + 16 * (u0 // SLOTS + 2), c + k,
                              h_hi[:, bass.ds(c + k, 1), :], TILES_IN)
                for c in range(FC - 2, FC):
                    u = u0 + 2 * c
                    chunk(u, u % SLOTS, 16 * (u // SLOTS + 2), c, h_hi[:, c, :], TILES_OUT)

            def output_chunk(n, j):
                if n + 1 < len(PHASES):
                    gained(n + 1, j, (x_ready, KC * n + j + 1))

            def ffn_out(n):
                u0 = UNIT0[n] + IN_UNITS[FFN]
                last = n + 1 == len(PHASES)

                with act.Fori(0, KC - 2, 2) as j:
                    for k in range(2):
                        if not last:
                            act.wait_ge(x_ready, j + (KC * n + k + 1))
                            nc.scalar.activation(xg_hi[:, bass.ds(j + k, 1), :], x[:, bass.ds(j + k, 1), :], ACT.Copy,
                                                 scale=gain[:, n + 1, bass.ds(j + k, 1)]).then_inc(xg_hi_ready, 1)
                        for i in range(2):
                            split_hi(j * 2 + (u0 + 2 * k + i + 1), 2 * k + i, TILES_OUT, j * 8 + 16 * (u0 // SLOTS + 2))
                for j in range(KC - 2, KC):
                    output_chunk(n, j)
                    if not last:
                        split_hi_at(u0 + 2 * j + 4, TILES_IN)
                        split_hi_at(u0 + 2 * j + 5, TILES_IN)

            def hi_part(source, k):
                nc.scalar.activation(h_hi[:, k, :], source, ACT.Copy).then_inc(h_hi_ready, 1)

            def mix(n):
                u0, p0 = UNIT0[n], PROJ0[n]

                def activate_v(c):
                    for t in range(TT):
                        act.wait_ge(proj_read, p0 + 2 * c + t + 1)
                        nc.scalar.activation(v_act[:, t, 256 * c:256 * c + 256], v_in[:, t, c, :],
                                             ACT.Gelu_apprx_tanh).then_inc(v_act_ready, 1)
                        act.wait_ge(v_act_ready, 2 * c + t + 1)
                        for g in (2 * c, 2 * c + 1):
                            i = N_GROUPS * t + g
                            nc.scalar.activation(v_in[:, t, c, P * (g % 2):P * (g % 2) + P], v_act[:, t, P * g:P * g + P], ACT.Square,
                                                 accum_out=v_ss[:, i:i + 1]).then_inc(v_ss_ready, 1)

                def activate_u(g):
                    act.wait_ge(proj_read, p0 + 8 + g + 1)
                    nc.scalar.activation(u_act[:, g % 2, :], u_in[:, g % 2, :],
                                         ACT.Gelu_apprx_tanh).then_inc(u_act_ready, 1)

                for s in range(12):
                    split_hi_at(u0 + s + 4, TILES_IN)
                    if s == 0:
                        root(n)
                    if s in (2, 3):
                        activate_v(s - 2)
                    if s == 4:
                        act.wait_ge(v_ms_ready, 1)
                        nc.scalar.activation(v_rms, v_ms, ACT.Sqrt).then_inc(v_rms_ready, 1)
                    if 6 <= s < 10:
                        at = SMALL_AT[("dft_pos", s - 6)]
                        act.wait_ge(small_done, at + 1)
                        hi_part(small[at % 2][:, 0:SEQ], s - 6)
                    if s >= 8:
                        activate_u(s - 8)
                    for g in GATES_AT.get(s, ()):
                        act.wait_ge(gated_ready, g + 1)
                        hi_part(gated, N_GROUPS + g)

            def att(n):
                u0, p0 = UNIT0[n], PROJ0[n]

                def squares(h):
                    act.wait_ge(proj_read, p0 + HEAD_UNIT[h] + 1)
                    if h >= 2:
                        act.wait_ge(small_done, SMALL_AT[("norm", h - 2)] + 1)
                    nc.scalar.activation(head_sq[:, h % 2, :], head_in[:, h % 3, :], ACT.Square).then_inc(head_sq_ready, 1)

                def head_root(h):
                    act.wait_ge(small_read, SMALL_AT[("norm", h)] + 1)
                    nc.scalar.activation(head_rms, head_ms, ACT.Sqrt).then_inc(head_rms_ready, 1)

                for s in range(len(ATT_HEAD_STEPS)):
                    if s < 12:
                        split_hi_at(u0 + s + 4, TILES_IN)
                    if s == 0:
                        root(n)
                    for kind, h in ATT_HEAD_STEPS[s]:
                        if kind == "scale":
                            squares(h)
                        if kind == "norm":
                            head_root(h)
                for h in range(N_HEADS + 2):
                    if h < N_HEADS:
                        act.wait_ge(max_ready, h + 1)
                        for t in range(TT):
                            e = nc.scalar.activation(probs[:, h % 2, t, :], proj[h % 4][:, SEQ * t:SEQ * t + SEQ], ACT.Exp,
                                                     bias=s_neg[:, h % 2, t:t + 1], accum_out=p_sum[:, h % 2, t:t + 1])
                        e.then_inc(probs_ready, 1)
                    if h >= 2:
                        act.wait_ge(ctx_done, h - 1)
                        hi_part(small[h % 2][:, 0:SEQ], h - 2)

            split_hi_at(0, TILES_IN)
            act.wait_ge(gains_loaded, 16)
            for k in range(KC):
                gained(0, k, (x_loaded[k // 4], 16))
            for s in range(1, SLOTS):
                split_hi_at(s, TILES_IN)
            for n, kind in enumerate(PHASES):
                if kind == FFN:
                    ffn(n)
                    ffn_out(n)
                else:
                    {MIX: mix, ATT: att}[kind](n)
                    for j in range(KC):
                        output_chunk(n, j)
                        split_hi_at(UNIT0[n] + 12 + j + 4, TILES_IN)
            root(len(PHASES))

        @block.vector
        def _(dve):
            made = [0]

            def own(instruction):
                made[0] += 1
                instruction.then_inc(dve_step, 1)
                dve.wait_ge(dve_step, made[0])

            def split_lo(u, slot, tiles):
                source, hi, lo = unit(slot, tiles)
                dve.wait_ge(hi_ready, u)
                nc.vector.tensor_tensor(lo, source, hi.bitcast(F32), ALU.subtract).then_inc(lo_ready, 1)

            def split_lo_at(u, tiles):
                split_lo(u + 1, u % SLOTS, tiles)

            def gained_lo(n, k):
                dve.wait_ge(xg_hi_ready, KC * n + k + 1)
                nc.vector.scalar_tensor_tensor(out=xg_lo[:, k, :], in0=x[:, k, :], scalar=gain[:, n, k:k + 1],
                                               in1=xg_hi[:, k, :].bitcast(F32), op0=ALU.mult,
                                               op1=ALU.subtract).then_inc(xg_ready, 1)

            def small_bank(use):
                at = SMALL_AT[use]
                dve.wait_ge(small_done, at + 1)
                return small[at % 2]

            def norm(n):
                bank = small_bank(("rms", n))
                nc.vector.tensor_scalar(mean_sq[:], bank[:, 0:SEQ], 1.0 / D_MODEL, EPS, ALU.mult,
                                        ALU.add).then_inc(small_read, 1)
                dve.wait_ge(rms_ready, n + 1)
                nc.vector.reciprocal(rinv[:], rms[:]).then_inc(rinv_ready, 1)
                dve.wait_ge(rinv_ready, n + 1)

            def lo_part(source, k, at):
                dve.wait_ge(h_hi_ready, at + 1)
                return nc.vector.tensor_tensor(h_lo[:, k, :], source, h_hi[:, k, :].bitcast(F32), ALU.subtract)

            def ffn(n):
                u0, hi0 = UNIT0[n], h_hi0(n)
                norm(n)

                def chunk(done, slot, c, hi, lo, tiles, splits_last):
                    bank = slot
                    dve.wait_ge(unit_done, done + 1)
                    nc.vector.tensor_tensor(gate_in[:], proj[bank][:, 0:SEQ], rinv[:], ALU.mult).then_inc(proj_read, 1)
                    dve.wait_ge(unit_done, done + 2)
                    nc.vector.tensor_tensor(up_in[:], proj[bank + 1][:, 0:SEQ], rinv[:], ALU.mult).then_inc(proj_read, 1)
                    dve.wait_ge(gate_ready, c + FFN_AT[n] * FC + 1)
                    dve.wait_ge(proj_read, c * 2 + (PROJ0[n] + 2))
                    nc.vector.tensor_tensor(inner[:], gate_act[:], up_in[:], ALU.mult).then_inc(inner_ready, 1)
                    if not splits_last:
                        split_lo(done + SLOTS + 1, slot, tiles)
                    dve.wait_ge(h_hi_ready, c + hi0 + 1)
                    nc.vector.tensor_tensor(lo, inner[:], hi.bitcast(F32), ALU.subtract).then_inc(h_ready, 1)
                    if splits_last:
                        split_lo(done + SLOTS + 1, slot, tiles)
                    split_lo(done + SLOTS + 2, slot + 1, tiles)

                with dve.Fori(0, FC - 2, 2) as c:
                    for k in range(2):
                        at = bass.ds(c + k, 1)
                        chunk(c * 2 + (u0 + 2 * k), 2 * k, c + k, h_hi[:, at, :], h_lo[:, at, :], TILES_IN, False)
                for c in range(FC - 2, FC):
                    u = u0 + 2 * c
                    chunk(u, u % SLOTS, c, h_hi[:, c, :], h_lo[:, c, :], TILES_OUT, True)

            def ffn_out(n):
                u0 = UNIT0[n] + IN_UNITS[FFN]
                last = n + 1 == len(PHASES)

                def residual(done, at, bank):
                    dve.wait_ge(unit_done, done + 2)
                    nc.vector.scalar_tensor_tensor(out=x[:, at, :], in0=down[bank][:, 0:SEQ], scalar=0.5,
                                                   in1=x[:, at, :], op0=ALU.mult, op1=ALU.add).then_inc(x_ready, 1)

                with dve.Fori(0, KC - 2, 2) as j:
                    for k in range(2):
                        at = bass.ds(j + k, 1)
                        residual(j * 2 + (u0 + 2 * k), at, k)
                        if not last:
                            dve.wait_ge(xg_hi_ready, j + (KC * (n + 1) + k + 1))
                            nc.vector.scalar_tensor_tensor(
                                out=xg_lo[:, at, :], in0=x[:, at, :], scalar=gain[:, n + 1, at],
                                in1=xg_hi[:, at, :].bitcast(F32), op0=ALU.mult, op1=ALU.subtract).then_inc(xg_ready, 1)
                        for i in range(2):
                            split_lo(j * 2 + (u0 + 2 * k + i + SLOTS + 1), 2 * k + i, TILES_OUT)
                for j in range(KC - 2, KC):
                    residual(u0 + 2 * j, slice(j, j + 1), j % 2)
                    if not last:
                        gained_lo(n + 1, j)
                        split_lo_at(u0 + 2 * j + 4, TILES_IN)
                        split_lo_at(u0 + 2 * j + 5, TILES_IN)

            def turned_rinv(n):
                bank = small_bank(("rcol", n))
                nc.vector.tensor_copy(rcol[:], bank[:, 0:TT]).then_inc(small_read, 1)
                dve.wait_ge(small_read, SMALL_AT[("rcol", n)] + 1)

            def mix(n):
                u0, hi0 = UNIT0[n], h_hi0(n)

                def scaled(target, s):
                    dve.wait_ge(unit_done, u0 + s + 1)
                    nc.vector.tensor_tensor(target, proj[s % 4][:, 0:SEQ], rinv[:], ALU.mult).then_inc(proj_read, 1)

                def v_scaled(c):
                    dve.wait_ge(unit_done, u0 + 2 * c + 2)
                    for t in range(TT):
                        nc.vector.tensor_scalar(v_in[:, t, c, :], proj[2 * c + t][:, 0:SEQ], rcol[:, t:t + 1], None,
                                                ALU.mult).then_inc(proj_read, 1)

                def v_normalised():
                    dve.wait_ge(v_ss_ready, TT * N_GROUPS)
                    nc.vector.tensor_scalar(v_ms, v_ss, 1.0 / P, EPS, ALU.mult, ALU.add).then_inc(v_ms_ready, 1)
                    dve.wait_ge(v_rms_ready, 1)
                    own(nc.vector.reciprocal(v_rinv, v_rms))
                    for t in range(TT):
                        for g in range(N_GROUPS):
                            i = N_GROUPS * t + g
                            last = nc.vector.tensor_scalar(v_norm[:, t, P * g:P * g + P], v_act[:, t, P * g:P * g + P],
                                                           v_rinv[:, i:i + 1], None, ALU.mult)
                    last.then_inc(v_norm_ready, 1)

                def dft_ch_out(g):
                    bank = small_bank(("dft_ch", g))
                    nc.vector.tensor_copy(f_ch[:, g % 2, :], bank[:]).then_inc(small_read, 1)

                def dft_pos_out(g):
                    bank = small_bank(("dft_pos", g))
                    lo_part(bank[:, 0:SEQ], g, hi0 + g).then_inc(small_read, 1)

                def gate(g):
                    bank = small_bank(("spatial", g))
                    nc.vector.scalar_tensor_tensor(
                        out=s_gate, in0=bank[:, 0:SEQ], scalar=head_gain[:, GAIN_V + g:GAIN_V + g + 1],
                        in1=b_s[:, g, :, :].rearrange("p t q -> p (t q)"), op0=ALU.mult, op1=ALU.add
                    ).then_inc(small_read, 1)
                    dve.wait_ge(small_read, SMALL_AT[("spatial", g)] + 1)
                    dve.wait_ge(u_act_ready, g + 1)
                    nc.vector.tensor_tensor(gated, u_act[:, g % 2, :], s_gate, ALU.mult).then_inc(gated_ready, 1)
                    lo_part(gated, N_GROUPS + g, hi0 + N_GROUPS + g).then_inc(h_ready, 1)

                for s in range(12):
                    if s == 0:
                        dve.wait_ge(tables_loaded, 16 * N_TABLES)
                        norm(n)
                    if s == 2:
                        turned_rinv(n)
                    if s in (2, 3):
                        v_scaled(s - 2)
                    if 4 <= s < 8:
                        scaled(f_in[:, s % 2, :], s)
                    if s >= 8:
                        scaled(u_in[:, s % 2, :], s)
                    if s == 4:
                        v_normalised()
                    if 6 <= s < 10:
                        dft_pos_out(s - 6)
                    if 5 <= s < 9:
                        dft_ch_out(s - 5)
                    for g in GATES_AT.get(s, ()):
                        gate(g)
                    split_lo_at(u0 + s + 4, TILES_IN)

            def att(n):
                u0, hi0, p0 = UNIT0[n], h_hi0(n), PROJ0[n]

                def head_scaled(h):
                    s = HEAD_UNIT[h]
                    dve.wait_ge(unit_done, u0 + s + 1)
                    nc.vector.tensor_tensor(head_in[:, h % 3, :], proj[s % 4][:, 0:SEQ], rinv[:], ALU.mult).then_inc(proj_read, 1)

                def head_norm(h):
                    bank = small_bank(("norm", h))
                    k = h < N_KV
                    nc.vector.tensor_scalar(head_ms, bank[:, 0:SEQ], 1.0 / HEAD_DIM if k else 1.0,
                                            EPS if k else EPS * HEAD_DIM, ALU.mult, ALU.add).then_inc(small_read, 1)
                    dve.wait_ge(head_rms_ready, h + 1)
                    own(nc.vector.reciprocal(head_rinv, head_rms))
                    dve.wait_ge(proj_read, p0 + HEAD_UNIT[h] + 1)
                    g = GAIN_K if k else GAIN_Q
                    nc.vector.scalar_tensor_tensor(out=head_n[:, h % 3, :], in0=head_in[:, h % 3, :],
                                                   scalar=head_gain[:, g:g + 1], in1=head_rinv, op0=ALU.mult,
                                                   op1=ALU.mult).then_inc(head_n_ready, 1)

                def head_turn(h):
                    bank = small_bank(("turn", h))
                    if h:
                        dve.wait_ge(head_t_ready, h)
                    nc.vector.tensor_tensor(head_sin, bank[:, 0:SEQ], cos_sin[:, 1, :], ALU.mult).then_inc(small_read, 1)
                    dve.wait_ge(small_read, SMALL_AT[("turn", h)] + 1)
                    dve.wait_ge(head_cos_ready, h + 1)
                    nc.vector.tensor_tensor(head_t[:, h, :], head_sin, head_cos[:, h % 2, :], ALU.add).then_inc(head_t_ready, 1)

                for s in range(len(ATT_HEAD_STEPS)):
                    if s == 0:
                        norm(n)
                    if s == 2:
                        turned_rinv(n)
                    if s == 3:
                        dve.wait_ge(unit_done, u0 + 4)
                        for t in range(TT):
                            nc.vector.tensor_scalar(v_keys[:, t, :], proj[2 + t][:, 0:SEQ], rcol[:, t:t + 1], None,
                                                    ALU.mult).then_inc(proj_read, 1)
                    for kind, h in ATT_HEAD_STEPS[s]:
                        {"scale": head_scaled, "norm": head_norm, "turn": head_turn}[kind](h)
                    if s < 12:
                        split_lo_at(u0 + s + 4, TILES_IN)

                for h in range(N_HEADS + 2):
                    b = h % 2
                    if h < N_HEADS:
                        dve.wait_ge(scores_done, h + 1)
                        own(nc.vector.tensor_reduce(s_max[:, b, :], proj[h % 4][:].rearrange("p (t k) -> p t k", t=TT),
                                                    AX_X, ALU.max))
                        nc.vector.tensor_scalar(s_neg[:, b, :], s_max[:, b, :], -1.0, None, ALU.mult).then_inc(max_ready, 1)
                    if 1 <= h <= N_HEADS:
                        dve.wait_ge(turned, h)
                        if h >= 3:
                            dve.wait_ge(ctx_done, h - 2)
                        nc.vector.tensor_copy(probs_t[:, 1 - b, :, :].rearrange("p t q -> p (t q)"), down[1 - b][:]
                                              ).then_inc(probs_t_ready, 1)
                    if h >= 2:
                        lo_part(small[b][:, 0:SEQ], h - 2, hi0 + h - 2).then_inc(h_ready, 1)
                    if h < N_HEADS:
                        dve.wait_ge(probs_ready, h + 1)
                        own(nc.vector.reciprocal(p_inv[:, b, :], p_sum[:, b, :]))
                        for t in range(TT):
                            last = nc.vector.tensor_scalar(probs_n[:, b, t, :], probs[:, b, t, :], p_inv[:, b, t:t + 1],
                                                           None, ALU.mult)
                        last.then_inc(probs_n_ready, 1)

            split_lo_at(0, TILES_IN)
            dve.wait_ge(gains_loaded, 16)
            for k in range(KC):
                dve.wait_ge(x_loaded[k // 4], 16)
                gained_lo(0, k)
            for s in range(1, SLOTS):
                split_lo_at(s, TILES_IN)
            for n, kind in enumerate(PHASES):
                if kind == FFN:
                    ffn(n)
                    ffn_out(n)
                else:
                    {MIX: mix, ATT: att}[kind](n)
                    for j in range(KC):
                        dve.wait_ge(unit_done, UNIT0[n] + 12 + j + 1)
                        nc.vector.tensor_tensor(x[:, j, :], down[j % 2][:, 0:SEQ], x[:, j, :], ALU.add).then_inc(x_ready, 1)
                        gained_lo(n + 1, j)
                        split_lo_at(UNIT0[n] + 12 + j + 4, TILES_IN)
            n = len(PHASES)
            norm(n)
            for j in range(KC):
                nc.vector.scalar_tensor_tensor(out=head_t[:, j, :], in0=x[:, j, :], scalar=gain[:, n, j:j + 1],
                                               in1=rinv[:], op0=ALU.mult, op1=ALU.mult).then_inc(y_ready, 1)

        @block.tensor
        def _(pe):
            def split_product(target, stationary, moving, first, last):
                nc.tensor.matmul(target, stationary[0], moving[0], start=first, stop=False, skip_group_check=True)
                nc.tensor.matmul(target, stationary[0], moving[1], start=False, stop=False, skip_group_check=True)
                return nc.tensor.matmul(target, stationary[1], moving[0], start=False, stop=last, skip_group_check=True)

            def tile(slot, i, width=P):
                at = slice(i * width, (i + 1) * width)
                return w_hi[slot][:, at], w_lo[slot][:, at]

            def pair(hi, lo, k, at=slice(0, SEQ)):
                return hi[:, k, at], lo[:, k, at]

            def column_unit(ready, slot, bank, xg0=None):
                pe.wait_ge(lo_ready, ready)
                for k in range(KC):
                    if xg0 is not None:
                        pe.wait_ge(xg_ready, xg0 + k + 1)
                    last = split_product(proj[bank][:, 0:SEQ], tile(slot, k), pair(xg_hi, xg_lo, k), k == 0, k == KC - 1)
                last.then_inc(unit_done, 1)

            def small_bank(use):
                at = SMALL_AT[use]
                if at >= 2:
                    pe.wait_ge(small_read, at - 1)
                return small[at % 2]

            def sum_over_channels(n):
                bank = small_bank(("rms", n))
                pe.wait_ge(sumsq_step, SUMSQ_STEPS * (n + 1))
                if n == 0:
                    pe.wait_ge(ones_ready, 1)
                nc.tensor.matmul(bank[:, 0:SEQ], ones[:], sumsq[:], start=True, stop=True).then_inc(small_done, 1)

            def turn_rinv(n):
                bank = small_bank(("rcol", n))
                pe.wait_ge(rinv_ready, n + 1)
                pe.wait_ge(tables_loaded, 16 * N_TABLES)
                for t in range(TT):
                    last = nc.tensor.matmul(bank[:, t:t + 1], rinv[:, P * t:P * t + P], ident[:, 0:1], start=True, stop=True)
                last.then_inc(small_done, 1)

            def token_unit(u, half, banks, xg0=None):
                pe.wait_ge(lo_ready, u + 1)
                for i in range(KC // 2):
                    k = KC // 2 * half + i
                    if xg0 is not None:
                        pe.wait_ge(xg_ready, xg0 + k + 1)
                    for t in range(TT):
                        last = split_product(proj[banks + t][:, 0:2 * P], pair(xg_hi, xg_lo, k, slice(P * t, P * t + P)),
                                             tile(u % SLOTS, i, 2 * P), k == 0, k == KC - 1)
                last.then_inc(unit_done, 1)

            def ffn(n):
                u0, p0 = UNIT0[n], PROJ0[n]
                for u in range(SLOTS):
                    if p0:
                        pe.wait_ge(proj_read, p0 + u - 3)
                    column_unit(u0 + u + 1, u, u, KC * n if u == 0 else None)
                    if u == 0:
                        sum_over_channels(n)
                with pe.Fori(SLOTS, IN_UNITS[FFN], SLOTS) as u:
                    for s in range(SLOTS):
                        pe.wait_ge(proj_read, u + (p0 + s - 3))
                        column_unit(u + (u0 + s + 1), s, s)

            def ffn_out(n):
                u0, c0 = UNIT0[n] + IN_UNITS[FFN], h0(n)

                def chunk(j, b):
                    first = b == 0 and not isinstance(j, bass.RuntimeValue)
                    if not (n == 0 and isinstance(j, int)):
                        pe.wait_ge(x_ready, j + (KC * n + b - 1))
                    for half in range(2):
                        slot = 2 * b + half
                        pe.wait_ge(lo_ready, j * 2 + (u0 + slot + 1))
                        for i in range(TILES_OUT):
                            c = TILES_OUT * half + i
                            if first and (c == 0 or c >= FC - 2):
                                pe.wait_ge(h_ready, c0 + (FC - 2 if c == 0 else c + 1))
                            last = split_product(down[b][:, 0:SEQ], tile(slot, i), pair(h_hi, h_lo, c), c == 0, c == FC - 1)
                        last.then_inc(unit_done, 1)

                for b in range(2):
                    chunk(0, b)
                with pe.Fori(2, KC, 2) as j:
                    for b in range(2):
                        chunk(j, b)

            def out_units(n):
                u0, c0 = UNIT0[n] + 12, h0(n)
                h_waits = [(h_ready, c0 + k + 1) for k in range(KC)]
                if PHASES[n] == MIX:
                    h_waits = [(small_read, SMALL_AT[("dft_pos", g)] + 1) for g in range(N_GROUPS)]
                    h_waits += [(h_ready, c0 + g + 1) for g in range(N_GROUPS)]
                for j in range(KC):
                    pe.wait_ge(lo_ready, u0 + j + 1)
                    pe.wait_ge(x_ready, KC * n + j - 1)
                    for k in range(KC):
                        if j == 0:
                            pe.wait_ge(*h_waits[k])
                        last = split_product(down[j % 2][:, 0:SEQ], tile((u0 + j) % SLOTS, k), pair(h_hi, h_lo, k), k == 0, k == KC - 1)
                    last.then_inc(unit_done, 1)

            def mix(n):
                u0, p0 = UNIT0[n], PROJ0[n]

                def dft_ch(g):
                    bank = small_bank(("dft_ch", g))
                    pe.wait_ge(proj_read, p0 + 4 + g + 1)
                    for t in range(TT):
                        last = nc.tensor.matmul(bank[:, 2 * P * t:2 * P * t + 2 * P], f_in[:, g % 2, P * t:P * t + P], dft_c[:],
                                                start=True, stop=True)
                    last.then_inc(small_done, 1)

                def dft_pos(g):
                    bank = small_bank(("dft_pos", g))
                    pe.wait_ge(small_read, SMALL_AT[("dft_ch", g)] + 1)
                    for t in range(TT):
                        for part in range(2):
                            at = 2 * P * t + P * part
                            last = nc.tensor.matmul(bank[:, 0:SEQ], f_ch[:, g % 2, at:at + P], dft_p[:, t, part, :],
                                                    start=t + part == 0, stop=t + part == 2)
                    last.then_inc(small_done, 1)

                def spatial(g):
                    bank = small_bank(("spatial", g))
                    pe.wait_ge(v_norm_ready, 1)
                    for t in range(TT):
                        last = nc.tensor.matmul(bank[:, P * t:P * t + P], v_norm[:, t, P * g:P * g + P], w_s[:, g, :],
                                                start=True, stop=True)
                    last.then_inc(small_done, 1)

                for s in range(12):
                    if s < 4:
                        if s % 2 == 0:
                            pe.wait_ge(proj_read, p0 + s - 2)
                        token_unit(u0 + s, s % 2, s // 2 * 2, KC * n if s < 2 else None)
                    else:
                        pe.wait_ge(proj_read, p0 + s - 3)
                        column_unit(u0 + s + 1, s % 4, s % 4)
                    if s == 0:
                        sum_over_channels(n)
                    if s == 2:
                        turn_rinv(n)
                    if 6 <= s < 10:
                        dft_pos(s - 6)
                    if 5 <= s < 9:
                        dft_ch(s - 5)
                    for g in GATES_AT.get(s, ()):
                        spatial(g)

            def att(n):
                u0, p0 = UNIT0[n], PROJ0[n]

                def sum_squares(h):
                    bank = small_bank(("norm", h))
                    pe.wait_ge(head_sq_ready, h + 1)
                    nc.tensor.matmul(bank[:, 0:SEQ], ones[:], head_sq[:, h % 2, :], start=True, stop=True).then_inc(small_done, 1)

                def swap_pairs(h):
                    bank = small_bank(("turn", h))
                    pe.wait_ge(head_n_ready, h + 1)
                    nc.tensor.matmul(bank[:, 0:SEQ], swap, head_n[:, h % 3, :], start=True, stop=True).then_inc(small_done, 1)

                def scores(h):
                    pe.wait_ge(head_t_ready, N_KV + h + 1)
                    pe.wait_ge(proj_read, p0 + 12)
                    if h >= 4:
                        pe.wait_ge(probs_ready, h - 3)
                    for t in range(TT):
                        last = nc.tensor.matmul(proj[h % 4][:, SEQ * t:SEQ * t + SEQ], head_t[:, N_KV + h, P * t:P * t + P],
                                                head_t[:, h // (N_HEADS // N_KV), :], start=True, stop=True)
                    last.then_inc(scores_done, 1)

                def turn(h):
                    pe.wait_ge(probs_n_ready, h + 1)
                    if h >= 2:
                        pe.wait_ge(probs_t_ready, h - 1)
                    for kt in range(TT):
                        for t in range(TT):
                            last = nc.tensor.transpose(down[h % 2][:, SEQ * kt + P * t:SEQ * kt + P * t + P],
                                                       probs_n[:, h % 2, t, P * kt:P * kt + P], ident)
                    last.then_inc(turned, 1)

                def context(h):
                    pe.wait_ge(probs_t_ready, h + 1)
                    pe.wait_ge(small_read, SMALL_AT[("turn", HEADS - 1)] + 1)
                    if h >= 2:
                        pe.wait_ge(h_ready, h0(n) + h - 1)
                    kv = h // (N_HEADS // N_KV)
                    for kt in range(TT):
                        last = nc.tensor.matmul(small[h % 2][:, 0:SEQ], v_keys[:, kt, HEAD_DIM * kv:HEAD_DIM * kv + HEAD_DIM],
                                                probs_t[:, h % 2, kt, :], start=kt == 0, stop=kt == TT - 1)
                    last.then_inc(ctx_done, 1)

                for s in range(len(ATT_HEAD_STEPS)):
                    if s in (2, 3):
                        if s == 2:
                            pe.wait_ge(proj_read, p0)
                        token_unit(u0 + s, s - 2, 2)
                    elif s < 12:
                        pe.wait_ge(proj_read, p0 + s - 3)
                        column_unit(u0 + s + 1, s % 4, s % 4, KC * n if s == 0 else None)
                    if s == 0:
                        sum_over_channels(n)
                    if s == 2:
                        turn_rinv(n)
                    for kind, h in ATT_HEAD_STEPS[s]:
                        if kind == "norm":
                            sum_squares(h)
                        if kind == "turn":
                            swap_pairs(h)
                scores(0)
                for h in range(N_HEADS + 2):
                    if h + 1 < N_HEADS:
                        scores(h + 1)
                    if 1 <= h <= N_HEADS:
                        turn(h - 1)
                    if h >= 2:
                        context(h - 2)

            for n, kind in enumerate(PHASES):
                if kind == FFN:
                    ffn(n)
                    ffn_out(n)
                else:
                    {MIX: mix, ATT: att}[kind](n)
                    out_units(n)
            sum_over_channels(len(PHASES))


def tiles(w, k, columns):
    return w.reshape(k, P, -1, columns).transpose(2, 1, 0, 3).reshape(-1, P, k * columns)


def ffn_in_units(gate, up):
    both = np.stack([tiles(gate, KC, P), tiles(up, KC, P)], axis=1)
    return both.reshape(2 * FC, P, TILES_IN * P)


def ffn_out_units(w):
    halves = w.reshape(2, TILES_OUT, P, KC, P).transpose(3, 0, 2, 1, 4)
    return halves.reshape(2 * KC, P, TILES_OUT * P)


def token_units(w):
    return w.reshape(2, KC // 2, P, -1, 2 * P).transpose(3, 0, 2, 1, 4).reshape(-1, P, TILES_IN * P)


def dft_tables():
    c = 2 * np.pi * np.outer(np.arange(P), np.arange(P)) / P
    channels = np.concatenate([np.cos(c), np.sin(c)], axis=1) / np.sqrt(P)
    t = 2 * np.pi * np.outer(np.arange(SEQ), np.arange(SEQ)) / SEQ
    positions = np.stack([np.cos(t), -np.sin(t)], axis=1) / np.sqrt(SEQ)
    positions = positions.reshape(TT, P, 2, SEQ).transpose(1, 0, 2, 3)
    return channels.astype(np.float32), np.ascontiguousarray(positions.astype(np.float32))


def rope_table():
    per_axis = HEAD_DIM // 4
    freq = 10000.0 ** (-np.arange(per_axis) / per_axis)
    t = np.arange(SEQ)
    angle = np.concatenate([np.outer(freq, t // GRID_W), np.outer(freq, t % GRID_W)])
    cos, sin = np.repeat(np.cos(angle), 2, axis=0), np.repeat(np.sin(angle), 2, axis=0)
    sin[0::2] *= -1
    return np.ascontiguousarray(np.stack([cos, sin], axis=1).astype(np.float32))


def kernel(**inputs):
    import concourse.bacc as bacc
    from concourse.bass_utils import run_bass_kernel_spmd

    a = {name: np.asarray(value) for name, value in inputs.items()}
    ffns = [(a[f + "_w_gate"][layer], a[f + "_w_up"][layer], a[f + "_w_down"][layer])
            for layer in range(2) for f in ("ffn1", "ffn2")]
    w_in, w_qkv = a["ab_w_in"][0], a["attn_w_qkv"][0]
    f_end, u_end = N_GROUPS * P, 2 * N_GROUPS * P
    q_end, k_end = N_HEADS * HEAD_DIM, (N_HEADS + N_KV) * HEAD_DIM
    norms = [a[name][layer] for layer in range(2) for name in ("ffn1_norm", "mix_norm", "ffn2_norm")] + [a["final_norm"]]
    dft_channels, dft_positions = dft_tables()
    swap = np.eye(P, dtype=np.float32)[np.arange(P) ^ 1]
    arrays = {
        "x_t": a["x"][0].T.reshape(KC, P, SEQ).transpose(1, 0, 2),
        "ffn_in_w": np.concatenate([ffn_in_units(gate, up) for gate, up, _ in ffns]),
        "ffn_out_w": np.concatenate([ffn_out_units(down) for _, _, down in ffns]),
        "mix_w": np.concatenate([token_units(w_in[:, u_end:]), tiles(w_in[:, :f_end], KC, P),
                                 tiles(w_in[:, f_end:u_end], KC, P), tiles(a["ab_w_out"][0], KC, P)]),
        "attn_w": np.concatenate([tiles(w_qkv[:, q_end:k_end], KC, P), token_units(w_qkv[:, k_end:]),
                                  tiles(w_qkv[:, :q_end], KC, P), tiles(a["attn_w_o"][0], KC, P)]),
        "gains": np.stack([g.reshape(KC, P).T for g in norms], axis=1),
        "head_gains": np.stack([*a["ab_v_norm"][0], a["attn_q_norm"][0], a["attn_k_norm"][0]], axis=1),
        "spatial_w": a["ab_w_s"][0].transpose(2, 0, 1),
        "spatial_b": np.broadcast_to(a["ab_b_s"][0][None, :, None, :], (P, N_GROUPS, TT, P)),
        "dft_channels": dft_channels,
        "dft_positions": dft_positions,
        "rope": rope_table(),
        "matrices": np.stack([np.eye(P, dtype=np.float32), swap], axis=1),
    }
    arrays = {name: np.ascontiguousarray(value) for name, value in arrays.items()}
    nc = bacc.Bacc("TRN2", target_bir_lowering=False, num_devices=1)
    aps = {name: nc.dram_tensor(name, value.shape, F32, kind="ExternalInput").ap() for name, value in arrays.items()}
    out = nc.dram_tensor("out_t", (P, KC, SEQ), F32, kind="ExternalOutput").ap()
    trunk_program(nc, out=out, **aps)
    result = run_bass_kernel_spmd(nc, [arrays], core_ids=[0])
    y = result.results[0]["out_t"]
    return y.transpose(1, 0, 2).reshape(1, D_MODEL, SEQ).transpose(0, 2, 1)
```

```python
from contextlib import ExitStack

import numpy as np

import concourse.bass as bass
from concourse import mybir

F32 = mybir.dt.float32
F32R = mybir.dt.float32r
ALU = mybir.AluOpType
ACT = mybir.ActivationFunctionType
AX_X = mybir.AxisListType.X

P = 128
D_MODEL = 1024
SEQ = 256
D_FF = 2816
HEAD_DIM = 128
N_HEADS = 8
N_KV = 2
GRID_W = 64
EPS = 1e-6

KC = D_MODEL // P
FC = D_FF // P
TT = SEQ // P
N_GROUPS = 4

SLOTS = 4
TILES_IN = KC
TILES_OUT = FC // 2
UNIT_MAX = TILES_OUT * P
MIXER_FLOATS = 9744

FFN, MIX, ATT = "ffn", "mix", "att"
PHASES = [FFN, MIX, FFN, FFN, ATT, FFN]
IN_UNITS = {FFN: 2 * FC, MIX: 12, ATT: 12}
OUT_UNITS = {FFN: 2 * KC, MIX: KC, ATT: KC}


def before(counts, n):
    return sum(counts[k] for k in PHASES[:n])


UNIT0 = [before({k: IN_UNITS[k] + OUT_UNITS[k] for k in IN_UNITS}, n) for n in range(len(PHASES))]
PROJ0 = [before({FFN: 2 * FC, MIX: 12, ATT: TT}, n) for n in range(len(PHASES))]
ROOTS = [n for n in range(len(PHASES) + 1) if n == len(PHASES) or PHASES[n] != ATT]
FFN_AT = {n: PHASES[:n].count(FFN) for n in range(len(PHASES)) if PHASES[n] == FFN}
N_NORMS = len(PHASES) + 1
SUMSQ_STEPS = 2 * KC - 1

ROTATE, SCORE, TURN, CONTEXT = 5, 6, 7, 8
ATT_STEPS = N_HEADS + CONTEXT
TURN_IN_DOWN = 5


def head_in_step(s, lag):
    return [s - lag] if 0 <= s - lag < N_HEADS else []


HEADS = N_KV + N_HEADS

GATES_AT = {9: (0, 1), 10: (2,), 11: (3,)}

SMALL = []
for _n, _kind in enumerate(PHASES):
    SMALL.append(("rms", _n))
    if _kind == MIX:
        SMALL += [("mean_col", _n), ("dft_ch", 0)]
        for _g in range(1, N_GROUPS):
            SMALL += [("dft_pos", _g - 1), ("dft_ch", _g)]
        SMALL += [("dft_pos", N_GROUPS - 1)] + [("spatial", _g) for _g in range(N_GROUPS)]
    if _kind == ATT:
        SMALL += [("mean_col", _n), ("k_sum", 0), ("k_swap", 0), ("k_sum", 1), ("k_swap", 1)]
        for _s in range(ROTATE, ATT_STEPS):
            SMALL += [("rotate", h) for h in head_in_step(_s, ROTATE)] + [("context", h) for h in head_in_step(_s, CONTEXT)]
SMALL.append(("rms", len(PHASES)))
SMALL_AT = {use: i for i, use in enumerate(SMALL)}

GAIN_V, GAIN_Q, GAIN_K = 0, N_GROUPS, N_GROUPS + 1
N_HEAD_GAINS = N_GROUPS + 2
N_TABLES = 7


def trunk_program(nc, x_t, ffn_in_w, ffn_out_w, mix_w, attn_w, gains, head_gains, spatial_w,
                  spatial_b, dft_channels, dft_positions, rope, matrices, out):
    with ExitStack() as ctx:
        def sb(name, shape, dt=F32):
            return ctx.enter_context(nc.sbuf_tensor(name, shape, dt))

        def sem(name):
            return ctx.enter_context(nc.semaphore(name))

        raw = [sb(f"raw{s}", [P, UNIT_MAX]) for s in range(SLOTS)]
        w_hi = [sb(f"w_hi{s}", [P, UNIT_MAX], F32R) for s in range(SLOTS)]
        w_lo = [sb(f"w_lo{s}", [P, UNIT_MAX], F32R) for s in range(SLOTS)]
        x = sb("x", [P, KC, SEQ])
        xg_hi = sb("xg_hi", [P, KC, SEQ], F32R)
        xg_lo = sb("xg_lo", [P, KC, SEQ], F32R)
        h_hi = sb("h_hi", [P, FC, SEQ], F32R)
        h_lo = sb("h_lo", [P, FC, SEQ], F32R)
        square = sb("square", [P, SEQ])
        sumsq = sb("sumsq", [P, SEQ])
        mean_sq = sb("mean_sq", [P, SEQ])
        rms = sb("rms", [P, SEQ])
        rinv = sb("rinv", [P, SEQ])
        mean_col = sb("mean_col", [P, TT])
        rcol = sb("rcol", [P, TT])
        gate_in = sb("gate_in", [P, SEQ])
        gate_act = sb("gate_act", [P, SEQ])
        up_in = sb("up_in", [P, SEQ])
        inner = sb("inner", [P, SEQ])
        mixers = sb("mixers", [P, MIXER_FLOATS])

        def carve():
            at = [0]

            def part(*dims):
                start, at[0] = at[0], at[0] + int(np.prod(dims))
                flat = mixers[:, start:at[0]]
                if len(dims) == 1:
                    return flat
                if len(dims) == 2:
                    return flat.rearrange("p (a b) -> p a b", a=dims[0])
                return flat.rearrange("p (a b c) -> p a b c", a=dims[0], b=dims[1])
            return part

        part = carve()
        v_in = part(TT, 2, SEQ)
        v_act = part(TT, N_GROUPS * P)
        v_ss = part(TT * N_GROUPS)
        v_ms = part(TT * N_GROUPS)
        v_rinv = part(TT * N_GROUPS)
        v_norm = part(TT, N_GROUPS * P)
        f_in = part(2, SEQ)
        f_ch = part(2, TT * 2 * P)
        u_in = part(2, SEQ)
        u_act = part(2, SEQ)
        s_gate = part(SEQ)
        gated = part(SEQ)
        part = carve()
        head_raw = part(2, SEQ)
        head_sq = part(2, SEQ)
        head_cos = part(2, SEQ)
        head_sin = part(SEQ)
        k_ms = part(SEQ)
        k_rms = part(SEQ)
        k_rinv = part(SEQ)
        k_sum = part(SEQ)
        k_rot = part(N_KV, SEQ)
        q_rot = part(2, SEQ)
        q_ms = part(2, TT)
        q_rinv = part(2, TT)
        q_eps = part(TT)
        v_keys = part(TT, N_KV * HEAD_DIM)
        cos_k = part(SEQ)
        cos_q = part(SEQ)
        swap_k = part(P)
        swap_q = part(P)
        s_max = part(2, TT)
        s_bias = part(2, TT)
        p_sum = part(2, TT)
        p_inv = part(2, TT)
        probs = part(2, TT, SEQ)
        probs_n = part(2, TT, SEQ)
        probs_t = part(2, TT, SEQ)
        part = carve()
        y = part(KC, SEQ)
        gain = sb("gain", [P, N_NORMS, KC])
        head_gain = sb("head_gain", [P, N_HEAD_GAINS])
        w_s = sb("w_s", [P, N_GROUPS, P])
        b_s = sb("b_s", [P, N_GROUPS, TT, P])
        dft_c = sb("dft_c", [P, 2 * P])
        dft_p = sb("dft_p", [P, TT, 2, SEQ])
        cos_sin = sb("cos_sin", [P, 2, SEQ])
        ones = sb("ones", [P, P])
        minus_half = sb("minus_half", [P, TT * N_GROUPS])
        silu_table = sb("silu_table", [P, 1])
        mats = sb("mats", [P, 2, P])
        ident, swap = mats[:, 0, :], mats[:, 1, :]

        proj = [ctx.enter_context(nc.psum_tensor(f"proj{i}", [P, 512], F32)) for i in range(4)]
        down = [ctx.enter_context(nc.psum_tensor(f"down{i}", [P, 512], F32)) for i in range(2)]
        small = [ctx.enter_context(nc.psum_tensor(f"small{i}", [P, 512], F32)) for i in range(2)]

        raw_landed = [sem(f"raw_landed{s}") for s in range(SLOTS)]
        hi_ready = sem("hi_ready")
        lo_ready = sem("lo_ready")
        unit_done = sem("unit_done")
        proj_read = sem("proj_read")
        small_done = sem("small_done")
        small_read = sem("small_read")
        x_loaded = [sem(f"x_loaded{i}") for i in range(KC // 2)]
        first_landed = sem("first_landed")
        first_hi = sem("first_hi")
        first_lo = sem("first_lo")
        gains_loaded = sem("gains_loaded")
        tables_loaded = sem("tables_loaded")
        x_ready = sem("x_ready")
        xg_hi_ready = sem("xg_hi_ready")
        xg_ready = sem("xg_ready")
        sumsq_step = sem("sumsq_step")
        rms_ready = sem("rms_ready")
        gate_ready = sem("gate_ready")
        inner_ready = sem("inner_ready")
        h_hi_ready = sem("h_hi_ready")
        h_ready = sem("h_ready")
        dve_step = sem("dve_step")
        ones_ready = sem("ones_ready")
        rinv_ready = sem("rinv_ready")
        rcol_ready = sem("rcol_ready")
        v_act_ready = sem("v_act_ready")
        v_ss_ready = sem("v_ss_ready")
        v_ms_ready = sem("v_ms_ready")
        v_rinv_ready = sem("v_rinv_ready")
        v_norm_ready = sem("v_norm_ready")
        u_act_ready = sem("u_act_ready")
        gated_ready = sem("gated_ready")
        head_copied = sem("head_copied")
        rope_ready = sem("rope_ready")
        k_rms_ready = sem("k_rms_ready")
        q_ms_ready = sem("q_ms_ready")
        q_rinv_ready = sem("q_rinv_ready")
        head_cos_ready = sem("head_cos_ready")
        rot_ready = sem("rot_ready")
        scores_done = sem("scores_done")
        bias_ready = sem("bias_ready")
        probs_ready = sem("probs_ready")
        probs_n_ready = sem("probs_n_ready")
        turned = sem("turned")
        probs_t_ready = sem("probs_t_ready")
        ctx_done = sem("ctx_done")
        y_ready = sem("y_ready")
        out_written = sem("out_written")

        block = ctx.enter_context(nc.Block())

        def unit(slot, tiles):
            return raw[slot][:, 0:tiles * P], w_hi[slot][:, 0:tiles * P], w_lo[slot][:, 0:tiles * P]

        def h_hi0(n):
            return before({FFN: FC, MIX: KC, ATT: KC}, n)

        def h0(n):
            return before({FFN: FC, MIX: KC - N_GROUPS, ATT: 0}, n)

        @block.sync
        def _(sp):
            def load(slot, source, tiles, splits):
                if splits is not None:
                    sp.wait_ge(lo_ready, splits)
                sp.dma_start(raw[slot][:, 0:tiles * P], source).then_inc(raw_landed[slot], 16)

            tables = ((mats, matrices), (head_gain, head_gains), (w_s, spatial_w), (b_s, spatial_b),
                      (dft_c, dft_channels), (dft_p, dft_positions), (cos_sin, rope))
            assert len(tables) == N_TABLES
            for n, kind in enumerate(PHASES):
                if n == 1:
                    for target, table in tables:
                        sp.dma_start(target[:], table).then_inc(tables_loaded, 16)
                source = {FFN: ffn_in_w, MIX: mix_w, ATT: attn_w}[kind]
                row0 = IN_UNITS[FFN] * FFN_AT[n] if kind == FFN else 0
                count = IN_UNITS[kind] + (OUT_UNITS[kind] if kind != FFN else 0)
                first = 0
                if n == 0:
                    half = TILES_IN * P // 2
                    sp.dma_start(raw[0][:, 0:half], source[0][:, 0:half]).then_inc(first_landed, 16)
                    sp.dma_start(raw[0][:, half:2 * half], source[0][:, half:2 * half]).then_inc(raw_landed[0], 16)
                    for s in range(1, SLOTS):
                        load(s, source[s], TILES_IN, None)
                    first = SLOTS
                with sp.Fori(first, count - SLOTS + 1, SLOTS) as u:
                    for s in range(SLOTS):
                        load(s, source[bass.ds(u + row0 + s, 1), :, :].rearrange("u p n -> p (u n)"),
                             TILES_IN, u + UNIT0[n] + s - SLOTS + 1)
                if kind == FFN:
                    with sp.Fori(0, OUT_UNITS[FFN] - SLOTS + 1, SLOTS) as u:
                        for s in range(SLOTS):
                            row = u + OUT_UNITS[FFN] * FFN_AT[n] + s
                            load(s, ffn_out_w[bass.ds(row, 1), :, :].rearrange("u p n -> p (u n)"),
                                 TILES_OUT, u + UNIT0[n] + IN_UNITS[FFN] + s - SLOTS + 1)
            for j in range(KC):
                sp.wait_ge(y_ready, j + 1)
                sp.dma_start(out[:, j, :], y[:, j, :]).then_inc(out_written, 16)
            sp.wait_ge(out_written, 16 * KC)

        def turn_bank(h):
            return down[h % 2] if h < TURN_IN_DOWN else proj[h % 2]

        @block.gpsimd
        def _(pool):
            def sum_squares(n):
                at = SUMSQ_STEPS * n
                for k in range(KC):
                    if n:
                        pool.wait_ge(x_ready, KC * (n - 1) + k + 1)
                    elif k % 2 == 0:
                        pool.wait_ge(x_loaded[k // 2], 16)
                    if k == 0:
                        nc.gpsimd.tensor_tensor(sumsq[:], x[:, 0, :], x[:, 0, :], ALU.mult).then_inc(sumsq_step, 1)
                        at += 1
                        continue
                    pool.wait_ge(sumsq_step, at)
                    nc.gpsimd.tensor_tensor(square[:], x[:, k, :], x[:, k, :], ALU.mult).then_inc(sumsq_step, 1)
                    at += 1
                    pool.wait_ge(sumsq_step, at)
                    nc.gpsimd.tensor_tensor(sumsq[:], sumsq[:], square[:], ALU.add).then_inc(sumsq_step, 1)
                    at += 1

            def inverse_root(target, source, ready):
                n = source.shape[-1]
                nc.gpsimd.tensor_tensor(target, source, minus_half[:, 0:n], ALU.pow).then_inc(ready, 1)

            def invert_mean(n):
                pool.wait_ge(small_read, SMALL_AT[("mean_col", n)] + 1)
                inverse_root(rcol[:], mean_col[:], rcol_ready)

            def head_times_cos(i, table):
                pool.wait_ge(head_copied, i + 1)
                if i >= 2:
                    pool.wait_ge(rot_ready, i - 1)
                nc.gpsimd.tensor_tensor(head_cos[:, i % 2, :], head_raw[:, i % 2, :], table, ALU.mult).then_inc(head_cos_ready, 1)

            nc.gpsimd.memset(ones[:], 1.0).then_inc(ones_ready, 1)
            nc.gpsimd.memset(minus_half[:], -0.5).then_inc(ones_ready, 1)
            pool.wait_ge(ones_ready, 2)
            for n in range(N_NORMS):
                sum_squares(n)
                kind = PHASES[n] if n < len(PHASES) else None
                if kind == MIX:
                    invert_mean(n)
                    pool.wait_ge(v_ms_ready, 1)
                    inverse_root(v_rinv, v_ms, v_rinv_ready)
                if kind == ATT:
                    invert_mean(n)
                    pool.wait_ge(rope_ready, 4)
                    for h in range(N_KV):
                        head_times_cos(h, cos_k)
                    for h in range(N_HEADS):
                        head_times_cos(N_KV + h, cos_q)
                        pool.wait_ge(q_ms_ready, h + 1)
                        if h >= 2:
                            pool.wait_ge(probs_ready, h - 1)
                        inverse_root(q_rinv[:, h % 2, :], q_ms[:, h % 2, :], q_rinv_ready)

        @block.scalar
        def _(act):
            for i in range(KC // 2):
                act.dma_start(x[:, 2 * i:2 * i + 2, :], x_t[:, 2 * i:2 * i + 2, :]).then_inc(x_loaded[i], 16)
                if i == 0:
                    act.dma_start(gain[:], gains).then_inc(gains_loaded, 16)

            def split_hi(u, slot, tiles, landings):
                source, hi, _ = unit(slot, tiles)
                act.wait_ge(raw_landed[slot], landings)
                if u is not None:
                    act.wait_ge(unit_done, u)
                nc.scalar.activation(hi, source, ACT.Copy).then_inc(hi_ready, 1)

            def split_hi_at(u, tiles):
                split_hi(u - SLOTS + 1 if u >= SLOTS else None, u % SLOTS, tiles, 16 * (u // SLOTS + 1))

            def gained(n, k, wait):
                act.wait_ge(*wait)
                nc.scalar.activation(xg_hi[:, k, :], x[:, k, :], ACT.Copy,
                                     scale=gain[:, n, k:k + 1]).then_inc(xg_hi_ready, 1)

            def root(n):
                act.wait_ge(small_read, SMALL_AT[("rms", n)] + 1)
                nc.scalar.activation(rms[:], mean_sq[:], ACT.Sqrt).then_inc(rms_ready, 1)

            def load_silu_table(n):
                act.wait_ge(rms_ready, ROOTS.index(n) + 1)
                nc.scalar.activation(silu_table[:], rms[:, 0:1], ACT.Silu)

            def ffn(n):
                u0 = UNIT0[n]

                def chunk(done, slot, landings, c, at, tiles):
                    split_hi(done + 1, slot, tiles, landings)
                    act.wait_ge(proj_read, 2 * c + PROJ0[n] + 1)
                    nc.scalar.activation(gate_act[:], gate_in[:], ACT.Silu).then_inc(gate_ready, 1)
                    act.wait_ge(inner_ready, c + FFN_AT[n] * FC + 1)
                    nc.scalar.activation(at, inner[:], ACT.Copy).then_inc(h_hi_ready, 1)
                    split_hi(done + 2, slot + 1, tiles, landings)

                root(n)
                load_silu_table(n)
                with act.Fori(0, FC - 2, 2) as c:
                    for k in range(2):
                        chunk(c * 2 + (u0 + 2 * k), 2 * k, c * 8 + 16 * (u0 // SLOTS + 2), c + k,
                              h_hi[:, bass.ds(c + k, 1), :], TILES_IN)
                for c in range(FC - 2, FC):
                    u = u0 + 2 * c
                    chunk(u, u % SLOTS, 16 * (u // SLOTS + 2), c, h_hi[:, c, :], TILES_OUT)

            def output_chunk(n, j):
                if n + 1 < len(PHASES):
                    gained(n + 1, j, (x_ready, KC * n + j + 1))

            def ffn_out(n):
                u0 = UNIT0[n] + IN_UNITS[FFN]
                last = n + 1 == len(PHASES)

                with act.Fori(0, KC - 2, 2) as j:
                    for k in range(2):
                        if not last:
                            act.wait_ge(x_ready, j + (KC * n + k + 1))
                            nc.scalar.activation(xg_hi[:, bass.ds(j + k, 1), :], x[:, bass.ds(j + k, 1), :], ACT.Copy,
                                                 scale=gain[:, n + 1, bass.ds(j + k, 1)]).then_inc(xg_hi_ready, 1)
                        for i in range(2):
                            split_hi(j * 2 + (u0 + 2 * k + i + 1), 2 * k + i, TILES_OUT, j * 8 + 16 * (u0 // SLOTS + 2))
                for j in range(KC - 2, KC):
                    output_chunk(n, j)
                    if not last:
                        split_hi_at(u0 + 2 * j + 4, TILES_IN)
                        split_hi_at(u0 + 2 * j + 5, TILES_IN)

            def hi_part(source, k):
                nc.scalar.activation(h_hi[:, k, :], source, ACT.Copy).then_inc(h_hi_ready, 1)

            def mix(n):
                u0, p0 = UNIT0[n], PROJ0[n]

                def activate_v(c):
                    for t in range(TT):
                        act.wait_ge(proj_read, p0 + 2 * c + t + 1)
                        nc.scalar.activation(v_act[:, t, 256 * c:256 * c + 256], v_in[:, t, c, :],
                                             ACT.Gelu_apprx_tanh).then_inc(v_act_ready, 1)
                        act.wait_ge(v_act_ready, 2 * c + t + 1)
                        for g in (2 * c, 2 * c + 1):
                            i = N_GROUPS * t + g
                            nc.scalar.activation(v_in[:, t, c, P * (g % 2):P * (g % 2) + P], v_act[:, t, P * g:P * g + P], ACT.Square,
                                                 accum_out=v_ss[:, i:i + 1]).then_inc(v_ss_ready, 1)

                def activate_u(g):
                    act.wait_ge(proj_read, p0 + 8 + g + 1)
                    nc.scalar.activation(u_act[:, g % 2, :], u_in[:, g % 2, :],
                                         ACT.Gelu_apprx_tanh).then_inc(u_act_ready, 1)

                for s in range(12):
                    split_hi_at(u0 + s + 4, TILES_IN)
                    if s == 0:
                        root(n)
                    if s in (2, 3):
                        activate_v(s - 2)
                    if 6 <= s < 10:
                        at = SMALL_AT[("dft_pos", s - 6)]
                        act.wait_ge(small_done, at + 1)
                        hi_part(small[at % 2][:, 0:SEQ], s - 6)
                    if s >= 8:
                        activate_u(s - 8)
                    for g in GATES_AT.get(s, ()):
                        act.wait_ge(gated_ready, g + 1)
                        hi_part(gated, N_GROUPS + g)

            def att(n):
                u0 = UNIT0[n]

                def copy_head(i, bank):
                    if i >= 2:
                        last_use = ("k_swap", i - 2) if i - 2 < N_KV else ("rotate", i - 2 - N_KV)
                        act.wait_ge(small_done, SMALL_AT[last_use] + 1)
                        act.wait_ge(head_cos_ready, i - 1)
                    nc.scalar.activation(head_raw[:, i % 2, :], proj[bank][:, 0:SEQ], ACT.Copy)
                    nc.scalar.activation(head_sq[:, i % 2, :], proj[bank][:, 0:SEQ], ACT.Square).then_inc(head_copied, 1)

                def k_root(h):
                    act.wait_ge(small_read, SMALL_AT[("k_sum", h)] + 1)
                    nc.scalar.activation(k_rms, k_ms, ACT.Sqrt, scale=1.0 / HEAD_DIM).then_inc(k_rms_ready, 1)

                for s in range(ATT_STEPS):
                    if s < 12 and s not in (2, 3):
                        act.wait_ge(unit_done, u0 + s + 1)
                        copy_head(s if s < N_KV else s - 2, s % 2)
                    if s in (1, 3):
                        k_root(s // 2)
                    for h in head_in_step(s, SCORE):
                        act.wait_ge(bias_ready, h + 1)
                        for t in range(TT):
                            e = nc.scalar.activation(probs[:, h % 2, t, :], proj[2 + h % 2][:, SEQ * t:SEQ * t + SEQ],
                                                     ACT.Exp, scale=q_rinv[:, h % 2, t:t + 1],
                                                     bias=s_bias[:, h % 2, t:t + 1], accum_out=p_sum[:, h % 2, t:t + 1])
                        e.then_inc(probs_ready, 1)
                    for h in head_in_step(s, CONTEXT):
                        at = SMALL_AT[("context", h)]
                        act.wait_ge(small_done, at + 1)
                        hi_part(small[at % 2][:, 0:SEQ], h)
                    if s < 12:
                        split_hi_at(u0 + s + 4, TILES_IN)

            act.wait_ge(gains_loaded, 16)
            for q in range(KC // 2):
                if q == 0:
                    act.wait_ge(first_landed, 16)
                if q == 2:
                    act.wait_ge(raw_landed[0], 16)
                at = slice(2 * P * q, 2 * P * q + 2 * P)
                i = nc.scalar.activation(w_hi[0][:, at], raw[0][:, at], ACT.Copy)
                i.then_inc(first_hi if q < 3 else hi_ready, 1)
                gained(0, 2 * q, (x_loaded[q], 16))
                gained(0, 2 * q + 1, (x_loaded[q], 16))
            for s in range(1, SLOTS):
                split_hi_at(s, TILES_IN)
            for n, kind in enumerate(PHASES):
                if kind == FFN:
                    ffn(n)
                    ffn_out(n)
                else:
                    {MIX: mix, ATT: att}[kind](n)
                    for j in range(KC):
                        output_chunk(n, j)
                        split_hi_at(UNIT0[n] + 12 + j + 4, TILES_IN)
            root(len(PHASES))

        @block.vector
        def _(dve):
            made = [0]

            def own(instruction):
                made[0] += 1
                instruction.then_inc(dve_step, 1)
                dve.wait_ge(dve_step, made[0])

            def split_lo(u, slot, tiles):
                source, hi, lo = unit(slot, tiles)
                dve.wait_ge(hi_ready, u)
                nc.vector.tensor_tensor(lo, source, hi.bitcast(F32), ALU.subtract).then_inc(lo_ready, 1)

            def split_lo_at(u, tiles):
                split_lo(u + 1, u % SLOTS, tiles)

            def gained_lo(n, k):
                dve.wait_ge(xg_hi_ready, KC * n + k + 1)
                nc.vector.scalar_tensor_tensor(out=xg_lo[:, k, :], in0=x[:, k, :], scalar=gain[:, n, k:k + 1],
                                               in1=xg_hi[:, k, :].bitcast(F32), op0=ALU.mult,
                                               op1=ALU.subtract).then_inc(xg_ready, 1)

            def small_bank(use):
                at = SMALL_AT[use]
                dve.wait_ge(small_done, at + 1)
                return small[at % 2]

            def mean(n):
                bank = small_bank(("rms", n))
                nc.vector.tensor_scalar(mean_sq[:], bank[:, 0:SEQ], 1.0 / D_MODEL, EPS, ALU.mult,
                                        ALU.add).then_inc(small_read, 1)

            def norm(n):
                mean(n)
                dve.wait_ge(rms_ready, ROOTS.index(n) + 1)
                nc.vector.reciprocal(rinv[:], rms[:]).then_inc(rinv_ready, 1)
                dve.wait_ge(rinv_ready, ROOTS.index(n) + 1)

            def lo_part(source, k, at):
                dve.wait_ge(h_hi_ready, at + 1)
                return nc.vector.tensor_tensor(h_lo[:, k, :], source, h_hi[:, k, :].bitcast(F32), ALU.subtract)

            def ffn(n):
                u0, hi0 = UNIT0[n], h_hi0(n)
                norm(n)

                def chunk(done, slot, c, hi, lo, tiles, splits_last):
                    bank = slot
                    dve.wait_ge(unit_done, done + 1)
                    nc.vector.tensor_tensor(gate_in[:], proj[bank][:, 0:SEQ], rinv[:], ALU.mult).then_inc(proj_read, 1)
                    dve.wait_ge(unit_done, done + 2)
                    nc.vector.tensor_tensor(up_in[:], proj[bank + 1][:, 0:SEQ], rinv[:], ALU.mult).then_inc(proj_read, 1)
                    dve.wait_ge(gate_ready, c + FFN_AT[n] * FC + 1)
                    dve.wait_ge(proj_read, c * 2 + (PROJ0[n] + 2))
                    nc.vector.tensor_tensor(inner[:], gate_act[:], up_in[:], ALU.mult).then_inc(inner_ready, 1)
                    if not splits_last:
                        split_lo(done + SLOTS + 1, slot, tiles)
                    dve.wait_ge(h_hi_ready, c + hi0 + 1)
                    nc.vector.tensor_tensor(lo, inner[:], hi.bitcast(F32), ALU.subtract).then_inc(h_ready, 1)
                    if splits_last:
                        split_lo(done + SLOTS + 1, slot, tiles)
                    split_lo(done + SLOTS + 2, slot + 1, tiles)

                with dve.Fori(0, FC - 2, 2) as c:
                    for k in range(2):
                        at = bass.ds(c + k, 1)
                        chunk(c * 2 + (u0 + 2 * k), 2 * k, c + k, h_hi[:, at, :], h_lo[:, at, :], TILES_IN, False)
                for c in range(FC - 2, FC):
                    u = u0 + 2 * c
                    chunk(u, u % SLOTS, c, h_hi[:, c, :], h_lo[:, c, :], TILES_OUT, True)

            def ffn_out(n):
                u0 = UNIT0[n] + IN_UNITS[FFN]
                last = n + 1 == len(PHASES)

                def residual(done, at, bank):
                    dve.wait_ge(unit_done, done + 2)
                    nc.vector.scalar_tensor_tensor(out=x[:, at, :], in0=down[bank][:, 0:SEQ], scalar=0.5,
                                                   in1=x[:, at, :], op0=ALU.mult, op1=ALU.add).then_inc(x_ready, 1)

                with dve.Fori(0, KC - 2, 2) as j:
                    for k in range(2):
                        at = bass.ds(j + k, 1)
                        residual(j * 2 + (u0 + 2 * k), at, k)
                        if not last:
                            dve.wait_ge(xg_hi_ready, j + (KC * (n + 1) + k + 1))
                            nc.vector.scalar_tensor_tensor(
                                out=xg_lo[:, at, :], in0=x[:, at, :], scalar=gain[:, n + 1, at],
                                in1=xg_hi[:, at, :].bitcast(F32), op0=ALU.mult, op1=ALU.subtract).then_inc(xg_ready, 1)
                        for i in range(2):
                            split_lo(j * 2 + (u0 + 2 * k + i + SLOTS + 1), 2 * k + i, TILES_OUT)
                for j in range(KC - 2, KC):
                    residual(u0 + 2 * j, slice(j, j + 1), j % 2)
                    if not last:
                        gained_lo(n + 1, j)
                        split_lo_at(u0 + 2 * j + 4, TILES_IN)
                        split_lo_at(u0 + 2 * j + 5, TILES_IN)

            def take_mean_col(n):
                bank = small_bank(("mean_col", n))
                nc.vector.tensor_copy(mean_col[:], bank[:, 0:TT]).then_inc(small_read, 1)

            def mix(n):
                u0, hi0 = UNIT0[n], h_hi0(n)

                def scaled(target, s):
                    dve.wait_ge(unit_done, u0 + s + 1)
                    nc.vector.tensor_tensor(target, proj[s % 4][:, 0:SEQ], rinv[:], ALU.mult).then_inc(proj_read, 1)

                def v_scaled(c):
                    dve.wait_ge(unit_done, u0 + 2 * c + 2)
                    for t in range(TT):
                        nc.vector.tensor_scalar(v_in[:, t, c, :], proj[2 * c + t][:, 0:SEQ], rcol[:, t:t + 1], None,
                                                ALU.mult).then_inc(proj_read, 1)

                def v_normalised():
                    dve.wait_ge(v_ss_ready, TT * N_GROUPS)
                    nc.vector.tensor_scalar(v_ms, v_ss, 1.0 / P, EPS, ALU.mult, ALU.add).then_inc(v_ms_ready, 1)
                    dve.wait_ge(v_rinv_ready, 1)
                    for t in range(TT):
                        for g in range(N_GROUPS):
                            i = N_GROUPS * t + g
                            last = nc.vector.tensor_scalar(v_norm[:, t, P * g:P * g + P], v_act[:, t, P * g:P * g + P],
                                                           v_rinv[:, i:i + 1], None, ALU.mult)
                    last.then_inc(v_norm_ready, 1)

                def dft_ch_out(g):
                    bank = small_bank(("dft_ch", g))
                    nc.vector.tensor_copy(f_ch[:, g % 2, :], bank[:]).then_inc(small_read, 1)

                def dft_pos_out(g):
                    bank = small_bank(("dft_pos", g))
                    lo_part(bank[:, 0:SEQ], g, hi0 + g).then_inc(small_read, 1)

                def gate(g):
                    bank = small_bank(("spatial", g))
                    nc.vector.scalar_tensor_tensor(
                        out=s_gate, in0=bank[:, 0:SEQ], scalar=head_gain[:, GAIN_V + g:GAIN_V + g + 1],
                        in1=b_s[:, g, :, :].rearrange("p t q -> p (t q)"), op0=ALU.mult, op1=ALU.add
                    ).then_inc(small_read, 1)
                    dve.wait_ge(small_read, SMALL_AT[("spatial", g)] + 1)
                    dve.wait_ge(u_act_ready, g + 1)
                    nc.vector.tensor_tensor(gated, u_act[:, g % 2, :], s_gate, ALU.mult).then_inc(gated_ready, 1)
                    lo_part(gated, N_GROUPS + g, hi0 + N_GROUPS + g).then_inc(h_ready, 1)

                for s in range(12):
                    if s == 0:
                        dve.wait_ge(tables_loaded, 16 * N_TABLES)
                        norm(n)
                    if s == 1:
                        take_mean_col(n)
                        dve.wait_ge(rcol_ready, 1)
                    if s in (2, 3):
                        v_scaled(s - 2)
                    if 4 <= s < 8:
                        scaled(f_in[:, s % 2, :], s)
                    if s >= 8:
                        scaled(u_in[:, s % 2, :], s)
                    if s == 4:
                        v_normalised()
                    if 6 <= s < 10:
                        dft_pos_out(s - 6)
                    if 5 <= s < 9:
                        dft_ch_out(s - 5)
                    for g in GATES_AT.get(s, ()):
                        gate(g)
                    split_lo_at(u0 + s + 4, TILES_IN)

            def att(n):
                u0, hi0 = UNIT0[n], h_hi0(n)

                def gained_tables():
                    dve.wait_ge(tables_loaded, 16 * N_TABLES)
                    for table, swapped, g in ((cos_k, swap_k, GAIN_K), (cos_q, swap_q, GAIN_Q)):
                        gain_ = head_gain[:, g:g + 1]
                        nc.vector.tensor_scalar(table, cos_sin[:, 0, :], gain_, None, ALU.mult).then_inc(rope_ready, 1)
                        nc.vector.tensor_scalar(swapped, swap, gain_, None, ALU.mult).then_inc(rope_ready, 1)

                def k_norm(h):
                    bank = small_bank(("k_sum", h))
                    nc.vector.scalar_tensor_tensor(out=k_ms, in0=mean_sq[:], scalar=EPS * HEAD_DIM, in1=bank[:, 0:SEQ],
                                                   op0=ALU.mult, op1=ALU.add).then_inc(small_read, 1)
                    dve.wait_ge(k_rms_ready, h + 1)
                    if h:
                        dve.wait_ge(rot_ready, h)
                    own(nc.vector.reciprocal(k_rinv, k_rms))

                def rotated(i, bank, target, read):
                    if i:
                        dve.wait_ge(rot_ready, i)
                    first = nc.vector.tensor_tensor(head_sin, bank[:, 0:SEQ], cos_sin[:, 1, :], ALU.mult)
                    first.then_inc(small_read, 1)
                    dve.wait_ge(small_read, read)
                    dve.wait_ge(head_cos_ready, i + 1)
                    return nc.vector.tensor_tensor(target, head_sin, head_cos[:, i % 2, :], ALU.add)

                def rotate_key(h):
                    bank = small_bank(("k_swap", h))
                    own(rotated(h, bank, k_sum, SMALL_AT[("k_swap", h)] + 1))
                    nc.vector.tensor_tensor(k_rot[:, h, :], k_sum, k_rinv, ALU.mult).then_inc(rot_ready, 1)

                def rotate_query(h):
                    bank = small_bank(("rotate", h))
                    nc.vector.tensor_tensor(q_ms[:, h % 2, :], bank[:, SEQ:SEQ + TT], q_eps, ALU.add).then_inc(q_ms_ready, 1)
                    rotated(N_KV + h, bank, q_rot[:, h % 2, :], SMALL_AT[("rotate", h)] + 1).then_inc(rot_ready, 1)

                for s in range(ATT_STEPS):
                    if s == 0:
                        gained_tables()
                        mean(n)
                    if s == 1:
                        take_mean_col(n)
                        dve.wait_ge(small_read, SMALL_AT[("mean_col", n)] + 1)
                        own(nc.vector.tensor_scalar(q_eps, mean_col[:], EPS * HEAD_DIM, None, ALU.mult))
                        k_norm(0)
                    if s == 2:
                        rotate_key(0)
                    if s == 3:
                        k_norm(1)
                        rotate_key(1)
                        dve.wait_ge(rcol_ready, 2)
                        dve.wait_ge(unit_done, u0 + 4)
                        for t in range(TT):
                            nc.vector.tensor_scalar(v_keys[:, t, :], proj[2 + t][:, 0:SEQ], rcol[:, t:t + 1], None,
                                                    ALU.mult).then_inc(proj_read, 1)
                    for h in head_in_step(s, ROTATE):
                        rotate_query(h)
                    for h in head_in_step(s, SCORE):
                        b = h % 2
                        dve.wait_ge(scores_done, h + 1)
                        own(nc.vector.tensor_reduce(s_max[:, b, :], proj[2 + b][:].rearrange("p (t k) -> p t k", t=TT),
                                                    AX_X, ALU.max))
                        dve.wait_ge(q_rinv_ready, h + 1)
                        nc.vector.scalar_tensor_tensor(out=s_bias[:, b, :], in0=s_max[:, b, :], scalar=-1.0,
                                                       in1=q_rinv[:, b, :], op0=ALU.mult, op1=ALU.mult).then_inc(bias_ready, 1)
                    for h in head_in_step(s, TURN):
                        dve.wait_ge(turned, h + 1)
                        if h >= 2:
                            dve.wait_ge(small_done, SMALL_AT[("context", h - 2)] + 1)
                        nc.vector.tensor_copy(probs_t[:, h % 2, :, :].rearrange("p t q -> p (t q)"), turn_bank(h)[:]
                                              ).then_inc(probs_t_ready, 1)
                    if s < 12:
                        split_lo_at(u0 + s + 4, TILES_IN)
                    for h in head_in_step(s, SCORE):
                        b = h % 2
                        dve.wait_ge(probs_ready, h + 1)
                        own(nc.vector.reciprocal(p_inv[:, b, :], p_sum[:, b, :]))
                        for t in range(TT):
                            last = nc.vector.tensor_scalar(probs_n[:, b, t, :], probs[:, b, t, :], p_inv[:, b, t:t + 1],
                                                           None, ALU.mult)
                        last.then_inc(probs_n_ready, 1)
                    for h in head_in_step(s, CONTEXT):
                        bank = small_bank(("context", h))
                        lo_part(bank[:, 0:SEQ], h, hi0 + h).then_inc(small_read, 1)

            dve.wait_ge(gains_loaded, 16)
            for q in range(KC // 2):
                dve.wait_ge(*((first_hi, q + 1) if q < 3 else (hi_ready, 1)))
                at = slice(2 * P * q, 2 * P * q + 2 * P)
                i = nc.vector.tensor_tensor(w_lo[0][:, at], raw[0][:, at], w_hi[0][:, at].bitcast(F32), ALU.subtract)
                i.then_inc(first_lo if q < 3 else lo_ready, 1)
                dve.wait_ge(x_loaded[q], 16)
                gained_lo(0, 2 * q)
                gained_lo(0, 2 * q + 1)
            for s in range(1, SLOTS):
                split_lo_at(s, TILES_IN)
            for n, kind in enumerate(PHASES):
                if kind == FFN:
                    ffn(n)
                    ffn_out(n)
                else:
                    {MIX: mix, ATT: att}[kind](n)
                    for j in range(KC):
                        dve.wait_ge(unit_done, UNIT0[n] + 12 + j + 1)
                        nc.vector.tensor_tensor(x[:, j, :], down[j % 2][:, 0:SEQ], x[:, j, :], ALU.add).then_inc(x_ready, 1)
                        gained_lo(n + 1, j)
                        split_lo_at(UNIT0[n] + 12 + j + 4, TILES_IN)
            n = len(PHASES)
            norm(n)
            for j in range(KC):
                nc.vector.scalar_tensor_tensor(out=y[:, j, :], in0=x[:, j, :], scalar=gain[:, n, j:j + 1],
                                               in1=rinv[:], op0=ALU.mult, op1=ALU.mult).then_inc(y_ready, 1)

        @block.tensor
        def _(pe):
            def split_product(target, stationary, moving, first, last):
                nc.tensor.matmul(target, stationary[0], moving[0], start=first, stop=False, skip_group_check=True)
                nc.tensor.matmul(target, stationary[0], moving[1], start=False, stop=False, skip_group_check=True)
                return nc.tensor.matmul(target, stationary[1], moving[0], start=False, stop=last, skip_group_check=True)

            def tile(slot, i, width=P):
                at = slice(i * width, (i + 1) * width)
                return w_hi[slot][:, at], w_lo[slot][:, at]

            def pair(hi, lo, k, at=slice(0, SEQ)):
                return hi[:, k, at], lo[:, k, at]

            def column_unit(ready, slot, bank, xg0=None):
                if ready is not None:
                    pe.wait_ge(lo_ready, ready)
                for k in range(KC):
                    if ready is None and k % 2 == 0:
                        pe.wait_ge(*((first_lo, k // 2 + 1) if k < KC - 2 else (lo_ready, 1)))
                    if xg0 is not None:
                        pe.wait_ge(xg_ready, xg0 + k + 1)
                    last = split_product(proj[bank][:, 0:SEQ], tile(slot, k), pair(xg_hi, xg_lo, k), k == 0, k == KC - 1)
                last.then_inc(unit_done, 1)

            def small_bank(use):
                at = SMALL_AT[use]
                if at >= 2:
                    pe.wait_ge(small_read, at - 1)
                return small[at % 2]

            def sum_over_channels(n):
                bank = small_bank(("rms", n))
                pe.wait_ge(sumsq_step, SUMSQ_STEPS * (n + 1))
                if n == 0:
                    pe.wait_ge(ones_ready, 1)
                nc.tensor.matmul(bank[:, 0:SEQ], ones[:], sumsq[:], start=True, stop=True).then_inc(small_done, 1)

            def turn_mean(n):
                bank = small_bank(("mean_col", n))
                pe.wait_ge(small_read, SMALL_AT[("rms", n)] + 1)
                pe.wait_ge(tables_loaded, 16 * N_TABLES)
                for t in range(TT):
                    last = nc.tensor.matmul(bank[:, t:t + 1], mean_sq[:, P * t:P * t + P], ident[:, 0:1], start=True, stop=True)
                last.then_inc(small_done, 1)

            def token_unit(u, half, banks, xg0=None):
                pe.wait_ge(lo_ready, u + 1)
                for i in range(KC // 2):
                    k = KC // 2 * half + i
                    if xg0 is not None:
                        pe.wait_ge(xg_ready, xg0 + k + 1)
                    for t in range(TT):
                        last = split_product(proj[banks + t][:, 0:2 * P], pair(xg_hi, xg_lo, k, slice(P * t, P * t + P)),
                                             tile(u % SLOTS, i, 2 * P), k == 0, k == KC - 1)
                last.then_inc(unit_done, 1)

            def ffn(n):
                u0, p0 = UNIT0[n], PROJ0[n]
                for u in range(SLOTS):
                    if p0:
                        pe.wait_ge(proj_read, p0 + u - 3)
                    column_unit(u0 + u + 1 if u0 + u else None, u, u, KC * n if u == 0 else None)
                    if u == 0:
                        sum_over_channels(n)
                with pe.Fori(SLOTS, IN_UNITS[FFN], SLOTS) as u:
                    for s in range(SLOTS):
                        pe.wait_ge(proj_read, u + (p0 + s - 3))
                        column_unit(u + (u0 + s + 1), s, s)

            def ffn_out(n):
                u0, c0 = UNIT0[n] + IN_UNITS[FFN], h0(n)

                def chunk(j, b):
                    first = b == 0 and not isinstance(j, bass.RuntimeValue)
                    if not (n == 0 and isinstance(j, int)):
                        pe.wait_ge(x_ready, j + (KC * n + b - 1))
                    for half in range(2):
                        slot = 2 * b + half
                        pe.wait_ge(lo_ready, j * 2 + (u0 + slot + 1))
                        for i in range(TILES_OUT):
                            c = TILES_OUT * half + i
                            if first and (c == 0 or c >= FC - 2):
                                pe.wait_ge(h_ready, c0 + (FC - 2 if c == 0 else c + 1))
                            last = split_product(down[b][:, 0:SEQ], tile(slot, i), pair(h_hi, h_lo, c), c == 0, c == FC - 1)
                        last.then_inc(unit_done, 1)

                for b in range(2):
                    chunk(0, b)
                with pe.Fori(2, KC, 2) as j:
                    for b in range(2):
                        chunk(j, b)

            def out_chunks(n, ks):
                u0, c0 = UNIT0[n] + 12, h0(n)
                if PHASES[n] == MIX:
                    h_waits = [(small_read, SMALL_AT[("dft_pos", g)] + 1) for g in range(N_GROUPS)]
                    h_waits += [(h_ready, c0 + g + 1) for g in range(N_GROUPS)]
                else:
                    h_waits = [(small_read, SMALL_AT[("context", h)] + 1) for h in range(N_HEADS)]
                if 0 in ks:
                    pe.wait_ge(lo_ready, u0 + 2)
                    if PHASES[n] == ATT:
                        pe.wait_ge(probs_t_ready, TURN_IN_DOWN)
                for k in ks:
                    pe.wait_ge(*h_waits[k])
                    for j in range(2):
                        last = split_product(down[j][:, 0:SEQ], tile((u0 + j) % SLOTS, k), pair(h_hi, h_lo, k), k == 0, k == KC - 1)
                        if k == KC - 1:
                            last.then_inc(unit_done, 1)

            def out_units(n):
                u0 = UNIT0[n] + 12
                for j in range(2, KC):
                    pe.wait_ge(lo_ready, u0 + j + 1)
                    pe.wait_ge(x_ready, KC * n + j - 1)
                    for k in range(KC):
                        last = split_product(down[j % 2][:, 0:SEQ], tile((u0 + j) % SLOTS, k), pair(h_hi, h_lo, k), k == 0, k == KC - 1)
                    last.then_inc(unit_done, 1)

            def mix(n):
                u0, p0 = UNIT0[n], PROJ0[n]

                def dft_ch(g):
                    bank = small_bank(("dft_ch", g))
                    pe.wait_ge(proj_read, p0 + 4 + g + 1)
                    for t in range(TT):
                        last = nc.tensor.matmul(bank[:, 2 * P * t:2 * P * t + 2 * P], f_in[:, g % 2, P * t:P * t + P], dft_c[:],
                                                start=True, stop=True)
                    last.then_inc(small_done, 1)

                def dft_pos(g):
                    bank = small_bank(("dft_pos", g))
                    pe.wait_ge(small_read, SMALL_AT[("dft_ch", g)] + 1)
                    for t in range(TT):
                        for part in range(2):
                            at = 2 * P * t + P * part
                            last = nc.tensor.matmul(bank[:, 0:SEQ], f_ch[:, g % 2, at:at + P], dft_p[:, t, part, :],
                                                    start=t + part == 0, stop=t + part == 2)
                    last.then_inc(small_done, 1)

                def spatial(g):
                    bank = small_bank(("spatial", g))
                    pe.wait_ge(v_norm_ready, 1)
                    for t in range(TT):
                        last = nc.tensor.matmul(bank[:, P * t:P * t + P], v_norm[:, t, P * g:P * g + P], w_s[:, g, :],
                                                start=True, stop=True)
                    last.then_inc(small_done, 1)

                for s in range(12):
                    if s < 4:
                        if s % 2 == 0:
                            pe.wait_ge(proj_read, p0 + s - 2)
                        token_unit(u0 + s, s % 2, s // 2 * 2, KC * n if s < 2 else None)
                    else:
                        pe.wait_ge(proj_read, p0 + s - 3)
                        column_unit(u0 + s + 1, s % 4, s % 4)
                    if s == 0:
                        sum_over_channels(n)
                    if s == 1:
                        turn_mean(n)
                    if 6 <= s < 10:
                        dft_pos(s - 6)
                    if 5 <= s < 9:
                        dft_ch(s - 5)
                    for g in GATES_AT.get(s, ()):
                        spatial(g)
                out_chunks(n, range(KC))

            def att(n):
                u0, p0 = UNIT0[n], PROJ0[n]

                def sum_key_squares(h):
                    bank = small_bank(("k_sum", h))
                    pe.wait_ge(head_copied, h + 1)
                    nc.tensor.matmul(bank[:, 0:SEQ], ones[:], head_sq[:, h, :], start=True, stop=True).then_inc(small_done, 1)

                def swap_key_pairs(h):
                    bank = small_bank(("k_swap", h))
                    pe.wait_ge(head_copied, h + 1)
                    pe.wait_ge(rope_ready, 4)
                    nc.tensor.matmul(bank[:, 0:SEQ], swap_k, head_raw[:, h, :], start=True, stop=True).then_inc(small_done, 1)

                def rotate(h):
                    i = N_KV + h
                    bank = small_bank(("rotate", h))
                    pe.wait_ge(head_copied, i + 1)
                    nc.tensor.matmul(bank[:, 0:SEQ], swap_q, head_raw[:, i % 2, :], start=True, stop=True)
                    for t in range(TT):
                        last = nc.tensor.matmul(bank[:, SEQ + t:SEQ + t + 1], head_sq[:, i % 2, P * t:P * t + P], ones[:, 0:1],
                                                start=True, stop=True)
                    last.then_inc(small_done, 1)

                def scores(h):
                    pe.wait_ge(rot_ready, N_KV + h + 1)
                    if h >= 2:
                        pe.wait_ge(probs_ready, h - 1)
                    else:
                        pe.wait_ge(proj_read, p0 + TT)
                    for t in range(TT):
                        last = nc.tensor.matmul(proj[2 + h % 2][:, SEQ * t:SEQ * t + SEQ], q_rot[:, h % 2, P * t:P * t + P],
                                                k_rot[:, h // (N_HEADS // N_KV), :], start=True, stop=True)
                    last.then_inc(scores_done, 1)

                def turn(h):
                    pe.wait_ge(probs_n_ready, h + 1)
                    if h >= 2:
                        pe.wait_ge(probs_t_ready, h - 1)
                    if h == TURN_IN_DOWN:
                        pe.wait_ge(head_copied, HEADS)
                    for kt in range(TT):
                        for t in range(TT):
                            at = SEQ * kt + P * t
                            last = nc.tensor.transpose(turn_bank(h)[:, at:at + P], probs_n[:, h % 2, t, P * kt:P * kt + P], ident)
                    last.then_inc(turned, 1)

                def context(h):
                    bank = small_bank(("context", h))
                    pe.wait_ge(probs_t_ready, h + 1)
                    kv = h // (N_HEADS // N_KV)
                    for kt in range(TT):
                        last = nc.tensor.matmul(bank[:, 0:SEQ], v_keys[:, kt, HEAD_DIM * kv:HEAD_DIM * kv + HEAD_DIM],
                                                probs_t[:, h % 2, kt, :], start=kt == 0, stop=kt == TT - 1)
                    last.then_inc(small_done, 1)

                out_between = {12: ((0,), (1,)), 13: ((2,), (3,)), 14: ((4,), (5,)), 15: ((6,), ())}
                for s in range(ATT_STEPS):
                    if s < 2:
                        column_unit(u0 + s + 1, s, s, KC * n if s == 0 else None)
                    elif s < 4:
                        token_unit(u0 + s, s - 2, 2)
                    elif s < 12:
                        pe.wait_ge(head_copied, s - 3)
                        column_unit(u0 + s + 1, s % 4, s % 2)
                    if s == 0:
                        sum_over_channels(n)
                    if s == 1:
                        turn_mean(n)
                        sum_key_squares(0)
                    if s == 2:
                        swap_key_pairs(0)
                        sum_key_squares(1)
                    if s == 3:
                        swap_key_pairs(1)
                    for h in head_in_step(s, ROTATE):
                        rotate(h)
                    for h in head_in_step(s, SCORE):
                        scores(h)
                    if s in out_between:
                        out_chunks(n, out_between[s][0])
                    for h in head_in_step(s, TURN):
                        turn(h)
                    if s in out_between:
                        out_chunks(n, out_between[s][1])
                    for h in head_in_step(s, CONTEXT):
                        context(h)
                out_chunks(n, (KC - 1,))

            for n, kind in enumerate(PHASES):
                if kind == FFN:
                    ffn(n)
                    ffn_out(n)
                else:
                    {MIX: mix, ATT: att}[kind](n)
                    out_units(n)
            sum_over_channels(len(PHASES))


def tiles(w, k, columns):
    return w.reshape(k, P, -1, columns).transpose(2, 1, 0, 3).reshape(-1, P, k * columns)


def ffn_in_units(gate, up):
    both = np.stack([tiles(gate, KC, P), tiles(up, KC, P)], axis=1)
    return both.reshape(2 * FC, P, TILES_IN * P)


def ffn_out_units(w):
    halves = w.reshape(2, TILES_OUT, P, KC, P).transpose(3, 0, 2, 1, 4)
    return halves.reshape(2 * KC, P, TILES_OUT * P)


def token_units(w):
    return w.reshape(2, KC // 2, P, -1, 2 * P).transpose(3, 0, 2, 1, 4).reshape(-1, P, TILES_IN * P)


def dft_tables():
    c = 2 * np.pi * np.outer(np.arange(P), np.arange(P)) / P
    channels = np.concatenate([np.cos(c), np.sin(c)], axis=1) / np.sqrt(P)
    t = 2 * np.pi * np.outer(np.arange(SEQ), np.arange(SEQ)) / SEQ
    positions = np.stack([np.cos(t), -np.sin(t)], axis=1) / np.sqrt(SEQ)
    positions = positions.reshape(TT, P, 2, SEQ).transpose(1, 0, 2, 3)
    return channels.astype(np.float32), np.ascontiguousarray(positions.astype(np.float32))


def rope_table():
    per_axis = HEAD_DIM // 4
    freq = 10000.0 ** (-np.arange(per_axis) / per_axis)
    t = np.arange(SEQ)
    angle = np.concatenate([np.outer(freq, t // GRID_W), np.outer(freq, t % GRID_W)])
    cos, sin = np.repeat(np.cos(angle), 2, axis=0), np.repeat(np.sin(angle), 2, axis=0)
    sin[0::2] *= -1
    return np.ascontiguousarray(np.stack([cos, sin], axis=1).astype(np.float32))


def kernel(**inputs):
    import concourse.bacc as bacc
    from concourse.bass_utils import run_bass_kernel_spmd

    a = {name: np.asarray(value) for name, value in inputs.items()}
    ffns = [(a[f + "_w_gate"][layer], a[f + "_w_up"][layer], a[f + "_w_down"][layer])
            for layer in range(2) for f in ("ffn1", "ffn2")]
    w_in, w_qkv = a["ab_w_in"][0], a["attn_w_qkv"][0]
    f_end, u_end = N_GROUPS * P, 2 * N_GROUPS * P
    q_end, k_end = N_HEADS * HEAD_DIM, (N_HEADS + N_KV) * HEAD_DIM
    norms = [a[name][layer] for layer in range(2) for name in ("ffn1_norm", "mix_norm", "ffn2_norm")] + [a["final_norm"]]
    dft_channels, dft_positions = dft_tables()
    swap = np.eye(P, dtype=np.float32)[np.arange(P) ^ 1]
    arrays = {
        "x_t": a["x"][0].T.reshape(KC, P, SEQ).transpose(1, 0, 2),
        "ffn_in_w": np.concatenate([ffn_in_units(gate, up) for gate, up, _ in ffns]),
        "ffn_out_w": np.concatenate([ffn_out_units(down) for _, _, down in ffns]),
        "mix_w": np.concatenate([token_units(w_in[:, u_end:]), tiles(w_in[:, :f_end], KC, P),
                                 tiles(w_in[:, f_end:u_end], KC, P), tiles(a["ab_w_out"][0], KC, P)]),
        "attn_w": np.concatenate([tiles(w_qkv[:, q_end:k_end], KC, P), token_units(w_qkv[:, k_end:]),
                                  tiles(w_qkv[:, :q_end], KC, P), tiles(a["attn_w_o"][0], KC, P)]),
        "gains": np.stack([g.reshape(KC, P).T for g in norms], axis=1),
        "head_gains": np.stack([*a["ab_v_norm"][0], a["attn_q_norm"][0], a["attn_k_norm"][0]], axis=1),
        "spatial_w": a["ab_w_s"][0].transpose(2, 0, 1),
        "spatial_b": np.broadcast_to(a["ab_b_s"][0][None, :, None, :], (P, N_GROUPS, TT, P)),
        "dft_channels": dft_channels,
        "dft_positions": dft_positions,
        "rope": rope_table(),
        "matrices": np.stack([np.eye(P, dtype=np.float32), swap], axis=1),
    }
    arrays = {name: np.ascontiguousarray(value) for name, value in arrays.items()}
    nc = bacc.Bacc("TRN2", target_bir_lowering=False, num_devices=1)
    aps = {name: nc.dram_tensor(name, value.shape, F32, kind="ExternalInput").ap() for name, value in arrays.items()}
    out = nc.dram_tensor("out_t", (P, KC, SEQ), F32, kind="ExternalOutput").ap()
    trunk_program(nc, out=out, **aps)
    result = run_bass_kernel_spmd(nc, [arrays], core_ids=[0])
    y = result.results[0]["out_t"]
    return y.transpose(1, 0, 2).reshape(1, D_MODEL, SEQ).transpose(0, 2, 1)
```

```python
from contextlib import ExitStack
from functools import partial

import numpy as np

import concourse.bass as bass
from concourse import mybir

F32 = mybir.dt.float32
F32R = mybir.dt.float32r
ALU = mybir.AluOpType
ACT = mybir.ActivationFunctionType
AX_X = mybir.AxisListType.X

P = 128
D_MODEL = 1024
SEQ = 256
D_FF = 2816
HEAD_DIM = 128
N_HEADS = 8
N_KV = 2
GRID_W = 64
EPS = 1e-6

KC = D_MODEL // P
FC = D_FF // P
TT = SEQ // P
N_GROUPS = 4

SLOTS = 4
TILES_IN = KC
TILES_OUT = FC // 2
UNIT_MAX = TILES_OUT * P
WARM_UP = 10
POOL_RESULTS = 6
MIXER_FLOATS = 8218

FFN, MIX, ATT = "ffn", "mix", "att"
PHASES = [FFN, MIX, FFN, FFN, ATT, FFN]
IN_UNITS = {FFN: 2 * FC, MIX: 12, ATT: 12}
OUT_UNITS = {FFN: 2 * KC, MIX: KC, ATT: KC}


def before(counts, n):
    return sum(counts[k] for k in PHASES[:n])


UNIT0 = [before({k: IN_UNITS[k] + OUT_UNITS[k] for k in IN_UNITS}, n) for n in range(len(PHASES))]
PROJ0 = [before({FFN: 2 * FC, MIX: 12, ATT: TT}, n) for n in range(len(PHASES))]
ROOTS = [n for n in range(len(PHASES) + 1) if n == len(PHASES) or PHASES[n] != ATT]
FFN_AT = {n: PHASES[:n].count(FFN) for n in range(len(PHASES)) if PHASES[n] == FFN}
N_NORMS = len(PHASES) + 1
SCALAR_SQUARES = KC // 2


def sumsq_steps(n):
    steps = [2 * KC - 1] * N_NORMS
    steps[0] -= SCALAR_SQUARES
    steps[-1] -= 2
    return sum(steps[:n])


ROTATE, SCORE, CONTEXT = 5, 6, 7
ATT_STEPS = N_HEADS + CONTEXT
TURN_IN_DOWN = 6


def head_in_step(s, lag):
    return [s - lag] if 0 <= s - lag < N_HEADS else []


HEADS = N_KV + N_HEADS

GATES_AT = {9: (0,), 10: (1, 2), 11: (3,)}

SMALL = []
for _n, _kind in enumerate(PHASES):
    SMALL.append(("rms", _n))
    if _kind == MIX:
        SMALL += [("mean_col", _n), ("dft_ch", 0)]
        for _g in range(1, N_GROUPS):
            SMALL += [("dft_pos", _g - 1), ("dft_ch", _g)]
        SMALL += [("dft_pos", N_GROUPS - 1)] + [("spatial", _g) for _g in range(N_GROUPS)]
    if _kind == ATT:
        SMALL += [("mean_col", _n), ("k_sum", 0), ("k_swap", 0), ("k_sum", 1), ("k_swap", 1)]
        for _s in range(ROTATE, ATT_STEPS):
            SMALL += [("rotate", h) for h in head_in_step(_s, ROTATE)] + [("context", h) for h in head_in_step(_s, CONTEXT)]
SMALL.append(("rms", len(PHASES)))
SMALL_AT = {use: i for i, use in enumerate(SMALL)}

GAIN_V, GAIN_Q, GAIN_K = 0, N_GROUPS, N_GROUPS + 1
N_HEAD_GAINS = N_GROUPS + 2
N_TABLES = 6


def trunk_program(nc, x_t, ffn_in_w, ffn_out_w, mix_w, attn_w, gains, head_gains, spatial_w,
                  spatial_b, dft_channels, dft_positions, rope, matrices, out):
    with ExitStack() as ctx:
        def sb(name, shape, dt=F32):
            return ctx.enter_context(nc.sbuf_tensor(name, shape, dt))

        def sem(name):
            return ctx.enter_context(nc.semaphore(name))

        raw = [sb(f"raw{s}", [P, UNIT_MAX]) for s in range(SLOTS)]
        w_hi = [sb(f"w_hi{s}", [P, UNIT_MAX], F32R) for s in range(SLOTS)]
        w_lo = [sb(f"w_lo{s}", [P, UNIT_MAX], F32R) for s in range(SLOTS)]
        x = sb("x", [P, KC, SEQ])
        xg_hi = sb("xg_hi", [P, KC, SEQ], F32R)
        xg_lo = sb("xg_lo", [P, KC, SEQ], F32R)
        h_hi = sb("h_hi", [P, FC, SEQ], F32R)
        h_lo = sb("h_lo", [P, FC, SEQ], F32R)
        square = sb("square", [P, SEQ])
        sumsq = sb("sumsq", [P, SEQ])
        mean_sq = sb("mean_sq", [P, SEQ])
        rms = sb("rms", [P, SEQ])
        rinv = sb("rinv", [P, SEQ])
        mean_col = sb("mean_col", [P, TT])
        rcol = sb("rcol", [P, TT])
        gate_in = sb("gate_in", [P, SEQ])
        gate_act = sb("gate_act", [P, SEQ])
        up_in = sb("up_in", [P, SEQ])
        inner = sb("inner", [P, SEQ])
        first_squares = [gate_in, gate_act, up_in, inner]
        mixers = sb("mixers", [P, MIXER_FLOATS])
        f_ch_hi = sb("f_ch_hi", [P, 2, TT * 2 * P], F32R)
        f_ch_lo = sb("f_ch_lo", [P, 2, TT * 2 * P], F32R)
        dft_p_hi = sb("dft_p_hi", [P, TT, 2, SEQ], F32R)
        dft_p_lo = sb("dft_p_lo", [P, TT, 2, SEQ], F32R)

        def carve():
            at = [0]

            def part(*dims):
                start, at[0] = at[0], at[0] + int(np.prod(dims))
                flat = mixers[:, start:at[0]]
                if len(dims) == 1:
                    return flat
                if len(dims) == 2:
                    return flat.rearrange("p (a b) -> p a b", a=dims[0])
                return flat.rearrange("p (a b c) -> p a b c", a=dims[0], b=dims[1])
            return part

        part = carve()
        v_in = part(TT, 2, SEQ)
        v_act = part(TT, N_GROUPS * P)
        v_ss = part(TT * N_GROUPS)
        v_ms = part(TT * N_GROUPS)
        v_rinv = part(TT * N_GROUPS)
        v_norm = part(TT, N_GROUPS * P)
        f_in = part(2, SEQ)
        u_in = part(2, SEQ)
        u_act = part(2, SEQ)
        s_gate = part(SEQ)
        gated = part(SEQ)
        part = carve()
        head_raw = part(2, SEQ)
        head_sq = part(2, SEQ)
        head_cos = part(2, SEQ)
        head_sin = part(SEQ)
        k_ms = part(SEQ)
        k_rms = part(SEQ)
        k_rinv = part(SEQ)
        k_sum = part(SEQ)
        k_rot = part(N_KV, SEQ)
        q_rot = part(2, SEQ)
        q_ms = part(2, TT)
        q_rinv = part(2, TT)
        q_eps = part(TT)
        v_keys = part(TT, N_KV * HEAD_DIM)
        cos_k = part(SEQ)
        cos_q = part(SEQ)
        swap_k = part(P)
        swap_q = part(P)
        s_max = part(2, TT)
        s_bias = part(2, TT)
        p_sum = part(2, TT)
        p_inv = part(2, TT)
        probs = part(2, TT, SEQ)
        probs_n = part(2, TT, SEQ)
        probs_t = part(2, TT, SEQ)
        part = carve()
        y = part(KC, SEQ)
        gain = sb("gain", [P, N_NORMS, KC])
        head_gain = sb("head_gain", [P, N_HEAD_GAINS])
        w_s = sb("w_s", [P, N_GROUPS, P])
        b_s = sb("b_s", [P, N_GROUPS, TT, P])
        dft_c = sb("dft_c", [P, 2 * P])
        dft_p = sb("dft_p", [P, TT, 2, SEQ])
        cos_sin = sb("cos_sin", [P, 2, SEQ])
        ones = sb("ones", [P, P])
        eps = sb("eps", [P, 1])
        minus_half = sb("minus_half", [P, TT * N_GROUPS])
        table_use = sb("table_use", [P, 2 * len(PHASES) + 3])
        mats = sb("mats", [P, 2, P])
        ident, swap = mats[:, 0, :], mats[:, 1, :]

        proj = [ctx.enter_context(nc.psum_tensor(f"proj{i}", [P, 512], F32)) for i in range(4)]
        down = [ctx.enter_context(nc.psum_tensor(f"down{i}", [P, 512], F32)) for i in range(2)]
        small = [ctx.enter_context(nc.psum_tensor(f"small{i}", [P, 512], F32)) for i in range(2)]

        raw_landed = [sem(f"raw_landed{s}") for s in range(SLOTS)]
        hi_ready = sem("hi_ready")
        lo_ready = sem("lo_ready")
        unit_done = sem("unit_done")
        proj_read = sem("proj_read")
        small_done = sem("small_done")
        small_read = sem("small_read")
        x_loaded = [sem(f"x_loaded{i}") for i in range(KC // 2)]
        first_landed = sem("first_landed")
        first_hi = sem("first_hi")
        first_lo = sem("first_lo")
        gains_loaded = sem("gains_loaded")
        tables_loaded = sem("tables_loaded")
        dft_p_loaded = sem("dft_p_loaded")
        x_ready = sem("x_ready")
        xg_hi_ready = sem("xg_hi_ready")
        xg_ready = sem("xg_ready")
        sumsq_step = sem("sumsq_step")
        square_ready = sem("square_ready")
        rms_ready = sem("rms_ready")
        gate_ready = sem("gate_ready")
        inner_ready = sem("inner_ready")
        h_hi_ready = sem("h_hi_ready")
        h_ready = sem("h_ready")
        dve_step = sem("dve_step")
        ones_ready = sem("ones_ready")
        rinv_ready = sem("rinv_ready")
        rcol_ready = sem("rcol_ready")
        dft_hi_ready = sem("dft_hi_ready")
        dft_lo_ready = sem("dft_lo_ready")
        v_act_ready = sem("v_act_ready")
        v_ss_ready = sem("v_ss_ready")
        v_ms_ready = sem("v_ms_ready")
        v_rinv_ready = sem("v_rinv_ready")
        v_norm_ready = sem("v_norm_ready")
        u_act_ready = sem("u_act_ready")
        gated_ready = sem("gated_ready")
        head_copied = sem("head_copied")
        rope_ready = sem("rope_ready")
        k_rms_ready = sem("k_rms_ready")
        q_ms_ready = sem("q_ms_ready")
        q_rinv_ready = sem("q_rinv_ready")
        head_cos_ready = sem("head_cos_ready")
        rot_ready = sem("rot_ready")
        scores_done = sem("scores_done")
        bias_ready = sem("bias_ready")
        probs_ready = sem("probs_ready")
        probs_n_ready = sem("probs_n_ready")
        turned = sem("turned")
        probs_t_ready = sem("probs_t_ready")
        y_ready = sem("y_ready")
        last_y_ready = sem("last_y_ready")
        out_written = sem("out_written")

        block = ctx.enter_context(nc.Block())

        def unit(slot, tiles):
            return raw[slot][:, 0:tiles * P], w_hi[slot][:, 0:tiles * P], w_lo[slot][:, 0:tiles * P]

        def h_hi0(n):
            return before({FFN: FC, MIX: KC, ATT: KC}, n)

        def h0(n):
            return before({FFN: FC, MIX: KC - N_GROUPS, ATT: 0}, n)

        @block.sync
        def _(sp):
            def load(slot, source, tiles, splits):
                if splits is not None:
                    sp.wait_ge(lo_ready, splits)
                sp.dma_start(raw[slot][:, 0:tiles * P], source).then_inc(raw_landed[slot], 16)

            tables = ((mats, matrices), (head_gain, head_gains), (w_s, spatial_w), (b_s, spatial_b),
                      (dft_c, dft_channels), (cos_sin, rope))
            assert len(tables) == N_TABLES
            for n, kind in enumerate(PHASES):
                if n == 1:
                    for target, table in tables:
                        sp.dma_start(target[:], table).then_inc(tables_loaded, 16)
                source = {FFN: ffn_in_w, MIX: mix_w, ATT: attn_w}[kind]
                row0 = IN_UNITS[FFN] * FFN_AT[n] if kind == FFN else 0
                count = IN_UNITS[kind] + (OUT_UNITS[kind] if kind != FFN else 0)
                first = 0
                if n == 0:
                    half = TILES_IN * P // 2
                    sp.dma_start(raw[0][:, 0:half], source[0][:, 0:half]).then_inc(first_landed, 16)
                    for i in range(KC // 2):
                        sp.dma_start(x[:, 2 * i:2 * i + 2, :], x_t[:, 2 * i:2 * i + 2, :]).then_inc(x_loaded[i], 16)
                        if i == 0:
                            sp.dma_start(raw[0][:, half:2 * half], source[0][:, half:2 * half]).then_inc(raw_landed[0], 16)
                    for s in range(1, SLOTS):
                        load(s, source[s], TILES_IN, None)
                    first = SLOTS
                with sp.Fori(first, count - SLOTS + 1, SLOTS) as u:
                    for s in range(SLOTS):
                        load(s, source[bass.ds(u + row0 + s, 1), :, :].rearrange("u p n -> p (u n)"),
                             TILES_IN, u + UNIT0[n] + s - SLOTS + 1)
                if n == 0:
                    sp.dma_start(dft_p[:], dft_positions).then_inc(dft_p_loaded, 16)
                if kind == FFN:
                    with sp.Fori(0, OUT_UNITS[FFN] - SLOTS + 1, SLOTS) as u:
                        for s in range(SLOTS):
                            row = u + OUT_UNITS[FFN] * FFN_AT[n] + s
                            load(s, ffn_out_w[bass.ds(row, 1), :, :].rearrange("u p n -> p (u n)"),
                                 TILES_OUT, u + UNIT0[n] + IN_UNITS[FFN] + s - SLOTS + 1)
            for j in range(0, KC, 2):
                sp.wait_ge(*((y_ready, j + 2) if j < POOL_RESULTS else (last_y_ready, j - POOL_RESULTS + 2)))
                sp.dma_start(out[:, j:j + 2, :], y[:, j:j + 2, :]).then_inc(out_written, 16)
            sp.wait_ge(out_written, 16 * (KC // 2))

        def turn_bank(h):
            return down[h % 2] if h < TURN_IN_DOWN else proj[h % 2]

        def out_bank(n, j):
            return proj[j] if j in (2, 3) else down[j % 2]

        def bank_before(j):
            return j - 4 if j < 6 else j - 2

        @block.gpsimd
        def _(pool):
            def sum_squares(n):
                at = sumsq_steps(n)
                for k in range(KC - 1 if n == len(PHASES) else KC):
                    if n:
                        pool.wait_ge(x_ready, KC * (n - 1) + k + 1)
                    elif k % 2 == 0:
                        pool.wait_ge(x_loaded[k // 2], 16)
                    if k == 0:
                        nc.gpsimd.tensor_tensor(sumsq[:], x[:, 0, :], x[:, 0, :], ALU.mult).then_inc(sumsq_step, 1)
                        at += 1
                        continue
                    pool.wait_ge(sumsq_step, at)
                    term = square
                    if n == 0 and k >= KC - SCALAR_SQUARES:
                        term = first_squares[k - KC + SCALAR_SQUARES]
                        pool.wait_ge(square_ready, k - KC + SCALAR_SQUARES + 1)
                    else:
                        nc.gpsimd.tensor_tensor(square[:], x[:, k, :], x[:, k, :], ALU.mult).then_inc(sumsq_step, 1)
                        at += 1
                        pool.wait_ge(sumsq_step, at)
                    nc.gpsimd.tensor_tensor(sumsq[:], sumsq[:], term[:], ALU.add).then_inc(sumsq_step, 1)
                    at += 1

            def inverse_root(target, source, ready):
                n = source.shape[-1]
                nc.gpsimd.tensor_tensor(target, source, minus_half[:, 0:n], ALU.pow).then_inc(ready, 1)

            def invert_mean(n):
                pool.wait_ge(small_read, SMALL_AT[("mean_col", n)] + 1)
                inverse_root(rcol[:], mean_col[:], rcol_ready)

            def head_times_cos(i, table):
                pool.wait_ge(head_copied, i + 1)
                if i >= 2:
                    pool.wait_ge(rot_ready, i - 1)
                nc.gpsimd.tensor_tensor(head_cos[:, i % 2, :], head_raw[:, i % 2, :], table, ALU.mult).then_inc(head_cos_ready, 1)

            nc.gpsimd.memset(ones[:], 1.0).then_inc(ones_ready, 1)
            nc.gpsimd.memset(minus_half[:], -0.5).then_inc(ones_ready, 1)
            nc.gpsimd.memset(eps[:], EPS).then_inc(ones_ready, 1)
            pool.wait_ge(ones_ready, 3)
            for n in range(N_NORMS):
                sum_squares(n)
                kind = PHASES[n] if n < len(PHASES) else None
                if kind == MIX:
                    invert_mean(n)
                    pool.wait_ge(v_ms_ready, 1)
                    inverse_root(v_rinv, v_ms, v_rinv_ready)
                if kind == ATT:
                    invert_mean(n)
                    pool.wait_ge(rope_ready, 4)
                    for h in range(N_KV):
                        head_times_cos(h, cos_k)
                    for h in range(N_HEADS):
                        head_times_cos(N_KV + h, cos_q)
                        pool.wait_ge(q_ms_ready, h + 1)
                        if h >= 2:
                            pool.wait_ge(probs_ready, h - 1)
                        inverse_root(q_rinv[:, h % 2, :], q_ms[:, h % 2, :], q_rinv_ready)
            pool.wait_ge(rinv_ready, len(ROOTS))
            for j in range(POOL_RESULTS, KC):
                nc.gpsimd.tensor_tensor(y[:, j, :], y[:, j, :], rinv[:], ALU.mult).then_inc(last_y_ready, 1)

        @block.scalar
        def _(act):
            act.dma_start(gain[:], gains).then_inc(gains_loaded, 16)
            act.wait_ge(ones_ready, 3)

            def split_hi(u, slot, tiles, landings):
                source, hi, _ = unit(slot, tiles)
                act.wait_ge(raw_landed[slot], landings)
                if u is not None:
                    act.wait_ge(unit_done, u)
                nc.scalar.activation(hi, source, ACT.Copy).then_inc(hi_ready, 1)

            def split_hi_at(u, tiles):
                split_hi(u - SLOTS + 1 if u >= SLOTS else None, u % SLOTS, tiles, 16 * (u // SLOTS + 1))

            def gained(n, k, wait):
                act.wait_ge(*wait)
                nc.scalar.activation(xg_hi[:, k, :], x[:, k, :], ACT.Copy,
                                     scale=gain[:, n, k:k + 1]).then_inc(xg_hi_ready, 1)

            def gained_or_result(n, at):
                last = n + 1 == len(PHASES)
                nc.scalar.activation((y if last else xg_hi)[:, at, :], x[:, at, :], ACT.Copy,
                                     scale=gain[:, n + 1, at]).then_inc(xg_hi_ready, 1)

            def root(n):
                act.wait_ge(small_read, SMALL_AT[("rms", n)] + 1)
                nc.scalar.activation(rms[:], mean_sq[:], ACT.Sqrt).then_inc(rms_ready, 1)

            tables_used = [0]

            def load_table(function):
                i = tables_used[0]
                tables_used[0] += 1
                nc.scalar.activation(table_use[:, i:i + 1], ones[:, 0:1], function)

            def ffn(n):
                u0 = UNIT0[n]

                def chunk(done, slot, landings, c, at, tiles):
                    split_hi(done + 1, slot, tiles, landings)
                    act.wait_ge(proj_read, 2 * c + PROJ0[n] + 1)
                    nc.scalar.activation(gate_act[:], gate_in[:], ACT.Silu).then_inc(gate_ready, 1)
                    act.wait_ge(inner_ready, c + FFN_AT[n] * FC + 1)
                    nc.scalar.activation(at, inner[:], ACT.Copy).then_inc(h_hi_ready, 1)
                    split_hi(done + 2, slot + 1, tiles, landings)

                root(n)
                load_table(ACT.Silu)
                with act.Fori(0, FC - 2, 2) as c:
                    for k in range(2):
                        chunk(c * 2 + (u0 + 2 * k), 2 * k, c * 8 + 16 * (u0 // SLOTS + 2), c + k,
                              h_hi[:, bass.ds(c + k, 1), :], TILES_IN)
                for c in range(FC - 2, FC):
                    u = u0 + 2 * c
                    chunk(u, u % SLOTS, 16 * (u // SLOTS + 2), c, h_hi[:, c, :], TILES_OUT)

            def output_chunk(n, j):
                act.wait_ge(x_ready, KC * n + j + 1)
                gained_or_result(n, slice(j, j + 1))

            def ffn_out(n):
                u0 = UNIT0[n] + IN_UNITS[FFN]
                last = n + 1 == len(PHASES)
                if last:
                    load_table(ACT.Sqrt)

                with act.Fori(0, KC - 2, 2) as j:
                    for k in range(2):
                        act.wait_ge(x_ready, j + (KC * n + k + 1))
                        gained_or_result(n, bass.ds(j + k, 1))
                        for i in range(2):
                            split_hi(j * 2 + (u0 + 2 * k + i + 1), 2 * k + i, TILES_OUT, j * 8 + 16 * (u0 // SLOTS + 2))
                if n == 0:
                    act.wait_ge(dft_p_loaded, 16)
                    nc.scalar.activation(dft_p_hi[:], dft_p[:], ACT.Copy).then_inc(dft_hi_ready, 1)
                for j in range(KC - 2, KC):
                    if last and j == KC - 1:
                        act.wait_ge(x_ready, KC * n + j + 1)
                        act.wait_ge(sumsq_step, sumsq_steps(N_NORMS))
                        nc.scalar.activation(square[:], x[:, j, :], ACT.Square).then_inc(square_ready, 1)
                    output_chunk(n, j)
                    if not last:
                        split_hi_at(u0 + 2 * j + 4, TILES_IN)
                        split_hi_at(u0 + 2 * j + 5, TILES_IN)

            def hi_part(source, k):
                nc.scalar.activation(h_hi[:, k, :], source, ACT.Copy).then_inc(h_hi_ready, 1)

            def mix(n):
                u0, p0 = UNIT0[n], PROJ0[n]

                def activate_v(c):
                    for t in range(TT):
                        act.wait_ge(proj_read, p0 + 2 * c + t + 1)
                        nc.scalar.activation(v_act[:, t, 256 * c:256 * c + 256], v_in[:, t, c, :],
                                             ACT.Gelu_apprx_tanh).then_inc(v_act_ready, 1)
                        act.wait_ge(v_act_ready, 2 * c + t + 1)
                        for g in (2 * c, 2 * c + 1):
                            i = N_GROUPS * t + g
                            nc.scalar.activation(v_in[:, t, c, P * (g % 2):P * (g % 2) + P], v_act[:, t, P * g:P * g + P], ACT.Square,
                                                 accum_out=v_ss[:, i:i + 1]).then_inc(v_ss_ready, 1)

                def activate_u(g):
                    act.wait_ge(proj_read, p0 + 8 + g + 1)
                    nc.scalar.activation(u_act[:, g % 2, :], u_in[:, g % 2, :],
                                         ACT.Gelu_apprx_tanh).then_inc(u_act_ready, 1)

                for s in range(12):
                    if s:
                        split_hi_at(u0 + s + 3, TILES_IN)
                    else:
                        root(n)
                    if s in (3, 5):
                        activate_v(s // 2 - 1)
                    if 6 <= s < 10:
                        at = SMALL_AT[("dft_pos", s - 6)]
                        act.wait_ge(small_done, at + 1)
                        hi_part(small[at % 2][:, 0:SEQ], s - 6)
                    if 5 <= s < 9:
                        at = SMALL_AT[("dft_ch", s - 5)]
                        act.wait_ge(small_done, at + 1)
                        nc.scalar.activation(f_ch_hi[:, (s - 5) % 2, :], small[at % 2][:], ACT.Copy).then_inc(dft_hi_ready, 1)
                    if s >= 8:
                        activate_u(s - 8)
                    for g in GATES_AT.get(s, ()):
                        act.wait_ge(gated_ready, g + 1)
                        hi_part(gated, N_GROUPS + g)
                split_hi_at(u0 + 15, TILES_IN)

            def att(n):
                u0 = UNIT0[n]

                def copy_head(i, bank):
                    if i >= 2:
                        last_use = ("k_swap", i - 2) if i - 2 < N_KV else ("rotate", i - 2 - N_KV)
                        act.wait_ge(small_done, SMALL_AT[last_use] + 1)
                        act.wait_ge(head_cos_ready, i - 1)
                    nc.scalar.activation(head_raw[:, i % 2, :], proj[bank][:, 0:SEQ], ACT.Copy)
                    nc.scalar.activation(head_sq[:, i % 2, :], proj[bank][:, 0:SEQ], ACT.Square).then_inc(head_copied, 1)

                def k_root(h):
                    act.wait_ge(small_read, SMALL_AT[("k_sum", h)] + 1)
                    nc.scalar.activation(k_rms, k_ms, ACT.Sqrt, scale=1.0 / HEAD_DIM).then_inc(k_rms_ready, 1)

                for s in range(ATT_STEPS + 1):
                    if s in (1, 2) or 5 <= s <= 12:
                        act.wait_ge(unit_done, u0 + s)
                        copy_head(s - 1 if s <= N_KV else s - 3, (s - 1) % 2)
                    if 1 <= s <= 12:
                        split_hi_at(u0 + s + 3, TILES_IN)
                    if s in (1, 3):
                        k_root(s // 2)
                    if s == 3:
                        load_table(ACT.Exp)
                    for h in head_in_step(s, CONTEXT + 1):
                        at = SMALL_AT[("context", h)]
                        act.wait_ge(small_done, at + 1)
                        hi_part(small[at % 2][:, 0:SEQ], h)
                    for h in head_in_step(s, SCORE):
                        act.wait_ge(bias_ready, h + 1)
                        for t in range(TT):
                            e = nc.scalar.activation(probs[:, h % 2, t, :], proj[2 + h % 2][:, SEQ * t:SEQ * t + SEQ],
                                                     ACT.Exp, scale=q_rinv[:, h % 2, t:t + 1],
                                                     bias=s_bias[:, h % 2, t:t + 1], accum_out=p_sum[:, h % 2, t:t + 1])
                        e.then_inc(probs_ready, 1)

            load_table(ACT.Sqrt)
            act.wait_ge(gains_loaded, 16)
            for q in range(KC // 2):
                if q == 0:
                    act.wait_ge(first_landed, 16)
                if q == 2:
                    act.wait_ge(raw_landed[0], 16)
                at = slice(2 * P * q, 2 * P * q + 2 * P)
                i = nc.scalar.activation(w_hi[0][:, at], raw[0][:, at], ACT.Copy)
                i.then_inc(first_hi if q < 3 else hi_ready, 1)
                gained(0, 2 * q, (x_loaded[q], 16))
                gained(0, 2 * q + 1, (x_loaded[q], 16))
            act.wait_ge(raw_landed[1], 16)
            half = TILES_IN * P // 2
            nc.scalar.activation(w_hi[1][:, 0:half], raw[1][:, 0:half], ACT.Copy).then_inc(first_hi, 1)
            nc.scalar.activation(w_hi[1][:, half:2 * half], raw[1][:, half:2 * half], ACT.Copy).then_inc(hi_ready, 1)
            for i in range(SCALAR_SQUARES):
                nc.scalar.activation(first_squares[i][:], x[:, KC - SCALAR_SQUARES + i, :], ACT.Square).then_inc(square_ready, 1)
            for s in range(2, SLOTS):
                split_hi_at(s, TILES_IN)
            for n, kind in enumerate(PHASES):
                if kind == FFN:
                    ffn(n)
                    ffn_out(n)
                else:
                    {MIX: mix, ATT: att}[kind](n)
                    for j in range(KC):
                        output_chunk(n, j)
                        split_hi_at(UNIT0[n] + 12 + j + 4, TILES_IN)
            n = len(PHASES)
            act.wait_ge(small_done, SMALL_AT[("rms", n)] + 1)
            nc.scalar.activation(rms[:], small[SMALL_AT[("rms", n)] % 2][:, 0:SEQ], ACT.Sqrt, scale=1.0 / D_MODEL,
                                 bias=eps[:, 0:1]).then_inc(rms_ready, 1)

        @block.vector
        def _(dve):
            made = [0]

            def own(instruction):
                made[0] += 1
                instruction.then_inc(dve_step, 1)
                dve.wait_ge(dve_step, made[0])

            def split_lo(u, slot, tiles):
                source, hi, lo = unit(slot, tiles)
                dve.wait_ge(hi_ready, u)
                nc.vector.tensor_tensor(lo, source, hi.bitcast(F32), ALU.subtract).then_inc(lo_ready, 1)

            def split_lo_at(u, tiles):
                split_lo(u + 1, u % SLOTS, tiles)

            def gained_lo(n, k):
                dve.wait_ge(xg_hi_ready, KC * n + k + 1)
                nc.vector.scalar_tensor_tensor(out=xg_lo[:, k, :], in0=x[:, k, :], scalar=gain[:, n, k:k + 1],
                                               in1=xg_hi[:, k, :].bitcast(F32), op0=ALU.mult,
                                               op1=ALU.subtract).then_inc(xg_ready, 1)

            def small_bank(use):
                at = SMALL_AT[use]
                dve.wait_ge(small_done, at + 1)
                return small[at % 2]

            def mean(n):
                bank = small_bank(("rms", n))
                nc.vector.tensor_scalar(mean_sq[:], bank[:, 0:SEQ], 1.0 / D_MODEL, EPS, ALU.mult,
                                        ALU.add).then_inc(small_read, 1)

            def norm(n):
                mean(n)
                dve.wait_ge(rms_ready, ROOTS.index(n) + 1)
                nc.vector.reciprocal(rinv[:], rms[:]).then_inc(rinv_ready, 1)
                dve.wait_ge(rinv_ready, ROOTS.index(n) + 1)

            def lo_part(source, k, at):
                dve.wait_ge(h_hi_ready, at + 1)
                return nc.vector.tensor_tensor(h_lo[:, k, :], source, h_hi[:, k, :].bitcast(F32), ALU.subtract)

            def ffn(n):
                u0, hi0 = UNIT0[n], h_hi0(n)
                norm(n)

                def chunk(done, slot, c, hi, lo, tiles, splits_last):
                    bank = slot
                    dve.wait_ge(unit_done, done + 1)
                    nc.vector.tensor_tensor(gate_in[:], proj[bank][:, 0:SEQ], rinv[:], ALU.mult).then_inc(proj_read, 1)
                    dve.wait_ge(unit_done, done + 2)
                    nc.vector.tensor_tensor(up_in[:], proj[bank + 1][:, 0:SEQ], rinv[:], ALU.mult).then_inc(proj_read, 1)
                    dve.wait_ge(gate_ready, c + FFN_AT[n] * FC + 1)
                    dve.wait_ge(proj_read, c * 2 + (PROJ0[n] + 2))
                    nc.vector.tensor_tensor(inner[:], gate_act[:], up_in[:], ALU.mult).then_inc(inner_ready, 1)
                    if not splits_last:
                        split_lo(done + SLOTS + 1, slot, tiles)
                    dve.wait_ge(h_hi_ready, c + hi0 + 1)
                    nc.vector.tensor_tensor(lo, inner[:], hi.bitcast(F32), ALU.subtract).then_inc(h_ready, 1)
                    if splits_last:
                        split_lo(done + SLOTS + 1, slot, tiles)
                    split_lo(done + SLOTS + 2, slot + 1, tiles)

                with dve.Fori(0, FC - 2, 2) as c:
                    for k in range(2):
                        at = bass.ds(c + k, 1)
                        chunk(c * 2 + (u0 + 2 * k), 2 * k, c + k, h_hi[:, at, :], h_lo[:, at, :], TILES_IN, False)
                for c in range(FC - 2, FC):
                    u = u0 + 2 * c
                    chunk(u, u % SLOTS, c, h_hi[:, c, :], h_lo[:, c, :], TILES_OUT, True)

            def ffn_out(n):
                u0 = UNIT0[n] + IN_UNITS[FFN]
                last = n + 1 == len(PHASES)

                def residual(done, at, bank):
                    dve.wait_ge(unit_done, done + 2)
                    nc.vector.scalar_tensor_tensor(out=x[:, at, :], in0=down[bank][:, 0:SEQ], scalar=0.5,
                                                   in1=x[:, at, :], op0=ALU.mult, op1=ALU.add).then_inc(x_ready, 1)

                with dve.Fori(0, KC - 2, 2) as j:
                    for k in range(2):
                        at = bass.ds(j + k, 1)
                        residual(j * 2 + (u0 + 2 * k), at, k)
                        if not last:
                            dve.wait_ge(xg_hi_ready, j + (KC * (n + 1) + k + 1))
                            nc.vector.scalar_tensor_tensor(
                                out=xg_lo[:, at, :], in0=x[:, at, :], scalar=gain[:, n + 1, at],
                                in1=xg_hi[:, at, :].bitcast(F32), op0=ALU.mult, op1=ALU.subtract).then_inc(xg_ready, 1)
                        for i in range(2):
                            split_lo(j * 2 + (u0 + 2 * k + i + SLOTS + 1), 2 * k + i, TILES_OUT)
                if n == 0:
                    dve.wait_ge(dft_hi_ready, 1)
                    nc.vector.tensor_tensor(dft_p_lo[:], dft_p[:], dft_p_hi[:].bitcast(F32), ALU.subtract).then_inc(dft_lo_ready, 1)
                for j in range(KC - 2, KC):
                    residual(u0 + 2 * j, slice(j, j + 1), j % 2)
                    if not last:
                        gained_lo(n + 1, j)
                        split_lo_at(u0 + 2 * j + 4, TILES_IN)
                        split_lo_at(u0 + 2 * j + 5, TILES_IN)

            def gained_tables():
                dve.wait_ge(tables_loaded, 16 * N_TABLES)
                for table, swapped, g in ((cos_k, swap_k, GAIN_K), (cos_q, swap_q, GAIN_Q)):
                    gain_ = head_gain[:, g:g + 1]
                    nc.vector.tensor_scalar(table, cos_sin[:, 0, :], gain_, None, ALU.mult).then_inc(rope_ready, 1)
                    nc.vector.tensor_scalar(swapped, swap, gain_, None, ALU.mult).then_inc(rope_ready, 1)

            def take_mean_col(n):
                bank = small_bank(("mean_col", n))
                nc.vector.tensor_copy(mean_col[:], bank[:, 0:TT]).then_inc(small_read, 1)

            def mix(n):
                u0, hi0 = UNIT0[n], h_hi0(n)

                def scaled(target, s):
                    dve.wait_ge(unit_done, u0 + s + 1)
                    nc.vector.tensor_tensor(target, proj[s % 4][:, 0:SEQ], rinv[:], ALU.mult).then_inc(proj_read, 1)

                def v_scaled(c):
                    dve.wait_ge(unit_done, u0 + 2 * c + 2)
                    for t in range(TT):
                        nc.vector.tensor_scalar(v_in[:, t, c, :], proj[2 * c + t][:, 0:SEQ], rcol[:, t:t + 1], None,
                                                ALU.mult).then_inc(proj_read, 1)

                def v_normalised():
                    dve.wait_ge(v_ss_ready, TT * N_GROUPS)
                    nc.vector.tensor_scalar(v_ms, v_ss, 1.0 / P, EPS, ALU.mult, ALU.add).then_inc(v_ms_ready, 1)
                    dve.wait_ge(v_rinv_ready, 1)
                    for t in range(TT):
                        for g in range(N_GROUPS):
                            i = N_GROUPS * t + g
                            last = nc.vector.tensor_scalar(v_norm[:, t, P * g:P * g + P], v_act[:, t, P * g:P * g + P],
                                                           v_rinv[:, i:i + 1], None, ALU.mult)
                    last.then_inc(v_norm_ready, 1)

                def dft_ch_out(g):
                    bank = small_bank(("dft_ch", g))
                    dve.wait_ge(dft_hi_ready, g + 2)
                    nc.vector.tensor_tensor(f_ch_lo[:, g % 2, :], bank[:], f_ch_hi[:, g % 2, :].bitcast(F32),
                                            ALU.subtract).then_inc(small_read, 1)

                def dft_pos_out(g):
                    bank = small_bank(("dft_pos", g))
                    lo_part(bank[:, 0:SEQ], g, hi0 + g).then_inc(small_read, 1)

                def gate(g):
                    bank = small_bank(("spatial", g))
                    nc.vector.scalar_tensor_tensor(
                        out=s_gate, in0=bank[:, 0:SEQ], scalar=head_gain[:, GAIN_V + g:GAIN_V + g + 1],
                        in1=b_s[:, g, :, :].rearrange("p t q -> p (t q)"), op0=ALU.mult, op1=ALU.add
                    ).then_inc(small_read, 1)
                    dve.wait_ge(small_read, SMALL_AT[("spatial", g)] + 1)
                    dve.wait_ge(u_act_ready, g + 1)
                    nc.vector.tensor_tensor(gated, u_act[:, g % 2, :], s_gate, ALU.mult).then_inc(gated_ready, 1)
                    lo_part(gated, N_GROUPS + g, hi0 + N_GROUPS + g).then_inc(h_ready, 1)

                for s in range(12):
                    if 0 < s < 11:
                        split_lo_at(u0 + s + 3, TILES_IN)
                    if s == 0:
                        dve.wait_ge(tables_loaded, 16 * N_TABLES)
                        norm(n)
                    if s == 1:
                        take_mean_col(n)
                        dve.wait_ge(rcol_ready, 1)
                    if s in (2, 3):
                        v_scaled(s - 2)
                    if 4 <= s < 8:
                        scaled(f_in[:, s % 2, :], s)
                    if s >= 8:
                        scaled(u_in[:, s % 2, :], s)
                    if 6 <= s < 10:
                        dft_pos_out(s - 6)
                    if 5 <= s < 9:
                        dft_ch_out(s - 5)
                    if s == 7:
                        v_normalised()
                    for g in GATES_AT.get(s, ()):
                        gate(g)
                split_lo_at(u0 + 14, TILES_IN)

            def att(n):
                u0, hi0 = UNIT0[n], h_hi0(n)

                def k_mean(h):
                    bank = small_bank(("k_sum", h))
                    nc.vector.scalar_tensor_tensor(out=k_ms, in0=mean_sq[:], scalar=EPS * HEAD_DIM, in1=bank[:, 0:SEQ],
                                                   op0=ALU.mult, op1=ALU.add).then_inc(small_read, 1)

                def k_inverse(h):
                    dve.wait_ge(k_rms_ready, h + 1)
                    if h:
                        dve.wait_ge(rot_ready, h)
                    own(nc.vector.reciprocal(k_rinv, k_rms))

                def rotated(i, bank, target, read):
                    if i:
                        dve.wait_ge(rot_ready, i)
                    first = nc.vector.tensor_tensor(head_sin, bank[:, 0:SEQ], cos_sin[:, 1, :], ALU.mult)
                    first.then_inc(small_read, 1)
                    dve.wait_ge(small_read, read)
                    dve.wait_ge(head_cos_ready, i + 1)
                    return nc.vector.tensor_tensor(target, head_sin, head_cos[:, i % 2, :], ALU.add)

                def rotate_key(h):
                    bank = small_bank(("k_swap", h))
                    own(rotated(h, bank, k_sum, SMALL_AT[("k_swap", h)] + 1))
                    nc.vector.tensor_tensor(k_rot[:, h, :], k_sum, k_rinv, ALU.mult).then_inc(rot_ready, 1)

                def rotate_query(h):
                    bank = small_bank(("rotate", h))
                    nc.vector.tensor_tensor(q_ms[:, h % 2, :], bank[:, SEQ:SEQ + TT], q_eps, ALU.add).then_inc(q_ms_ready, 1)
                    rotated(N_KV + h, bank, q_rot[:, h % 2, :], SMALL_AT[("rotate", h)] + 1).then_inc(rot_ready, 1)

                def row_maxima(h):
                    b = h % 2
                    dve.wait_ge(scores_done, h + 1)
                    own(nc.vector.tensor_reduce(s_max[:, b, :], proj[2 + b][:].rearrange("p (t k) -> p t k", t=TT),
                                                AX_X, ALU.max))
                    dve.wait_ge(q_rinv_ready, h + 1)
                    nc.vector.scalar_tensor_tensor(out=s_bias[:, b, :], in0=s_max[:, b, :], scalar=-1.0,
                                                   in1=q_rinv[:, b, :], op0=ALU.mult, op1=ALU.mult).then_inc(bias_ready, 1)

                def normalise(h):
                    b = h % 2
                    dve.wait_ge(probs_ready, h + 1)
                    own(nc.vector.reciprocal(p_inv[:, b, :], p_sum[:, b, :]))
                    for t in range(TT):
                        last = nc.vector.tensor_scalar(probs_n[:, b, t, :], probs[:, b, t, :], p_inv[:, b, t:t + 1],
                                                       None, ALU.mult)
                    last.then_inc(probs_n_ready, 1)

                def take_turned(h):
                    dve.wait_ge(turned, h + 1)
                    if h >= 2:
                        dve.wait_ge(small_done, SMALL_AT[("context", h - 2)] + 1)
                    nc.vector.tensor_copy(probs_t[:, h % 2, :, :].rearrange("p t q -> p (t q)"), turn_bank(h)[:]
                                          ).then_inc(probs_t_ready, 1)

                for s in range(ATT_STEPS + 1):
                    if s != 13:
                        for h in head_in_step(s, SCORE + 1):
                            take_turned(h)
                    for h in head_in_step(s, SCORE):
                        row_maxima(h)
                    if s == 13:
                        take_turned(s - SCORE - 1)
                    if s == 0:
                        mean(n)
                    for h in head_in_step(s, CONTEXT + 1):
                        bank = small_bank(("context", h))
                        lo_part(bank[:, 0:SEQ], h, hi0 + h).then_inc(small_read, 1)
                    if s in (5, 12):
                        rotate_query(s - ROTATE)
                    if s == 3:
                        k_mean(1)
                    if 1 <= s <= 12:
                        split_lo_at(u0 + s + 3, TILES_IN)
                    if s == 1:
                        take_mean_col(n)
                        dve.wait_ge(small_read, SMALL_AT[("mean_col", n)] + 1)
                        own(nc.vector.tensor_scalar(q_eps, mean_col[:], EPS * HEAD_DIM, None, ALU.mult))
                        k_mean(0)
                    if s in (1, 3):
                        k_inverse(s // 2)
                    if s in (2, 4):
                        rotate_key(s // 2 - 1)
                    if s == 4:
                        dve.wait_ge(rcol_ready, 2)
                        dve.wait_ge(unit_done, u0 + 4)
                        for t in range(TT):
                            nc.vector.tensor_scalar(v_keys[:, t, :], proj[2 + t][:, 0:SEQ], rcol[:, t:t + 1], None,
                                                    ALU.mult).then_inc(proj_read, 1)
                    for h in head_in_step(s, SCORE):
                        normalise(h)
                    if 5 < s < 12:
                        rotate_query(s - ROTATE)

            dve.wait_ge(gains_loaded, 16)
            for q in range(KC // 2):
                dve.wait_ge(*((first_hi, q + 1) if q < 3 else (hi_ready, 1)))
                at = slice(2 * P * q, 2 * P * q + 2 * P)
                i = nc.vector.tensor_tensor(w_lo[0][:, at], raw[0][:, at], w_hi[0][:, at].bitcast(F32), ALU.subtract)
                i.then_inc(first_lo if q < 3 else lo_ready, 1)
                dve.wait_ge(x_loaded[q], 16)
                gained_lo(0, 2 * q)
                gained_lo(0, 2 * q + 1)
            half = TILES_IN * P // 2
            dve.wait_ge(first_hi, KC // 2)
            nc.vector.tensor_tensor(w_lo[1][:, 0:half], raw[1][:, 0:half], w_hi[1][:, 0:half].bitcast(F32),
                                    ALU.subtract).then_inc(first_lo, 1)
            dve.wait_ge(hi_ready, 2)
            nc.vector.tensor_tensor(w_lo[1][:, half:2 * half], raw[1][:, half:2 * half], w_hi[1][:, half:2 * half].bitcast(F32),
                                    ALU.subtract).then_inc(lo_ready, 1)
            for s in range(2, SLOTS):
                split_lo_at(s, TILES_IN)
            for n, kind in enumerate(PHASES):
                if kind == FFN:
                    if PHASES[n + 1:n + 2] == [ATT]:
                        gained_tables()
                    ffn(n)
                    ffn_out(n)
                else:
                    {MIX: mix, ATT: att}[kind](n)
                    u0 = UNIT0[n] + 12
                    for j in range(KC):
                        for i in {0: (0, 1), 1: ()}.get(j, (j,)):
                            dve.wait_ge(unit_done, u0 + i + 1)
                            nc.vector.tensor_tensor(x[:, i, :], out_bank(n, i)[:, 0:SEQ], x[:, i, :],
                                                    ALU.add).then_inc(x_ready, 1)
                        if j < KC - 1 and not (kind == ATT and j == 0):
                            split_lo_at(u0 + j + 3, TILES_IN)
                        gained_lo(n + 1, j)
                    for j in range(KC - 1, KC + 1):
                        split_lo_at(u0 + j + 3, TILES_IN)
            dve.wait_ge(rms_ready, len(ROOTS))
            nc.vector.reciprocal(rinv[:], rms[:]).then_inc(rinv_ready, 1)
            dve.wait_ge(rinv_ready, len(ROOTS))
            dve.wait_ge(xg_hi_ready, KC * len(PHASES) + KC)
            for j in range(POOL_RESULTS):
                nc.vector.tensor_tensor(y[:, j, :], y[:, j, :], rinv[:], ALU.mult).then_inc(y_ready, 1)

        @block.tensor
        def _(pe):
            def split_product(target, stationary, moving, first, last):
                nc.tensor.matmul(target, stationary[0], moving[0], start=first, stop=False, skip_group_check=True)
                nc.tensor.matmul(target, stationary[0], moving[1], start=False, stop=False, skip_group_check=True)
                return nc.tensor.matmul(target, stationary[1], moving[0], start=False, stop=last, skip_group_check=True)

            def tile(slot, i, width=P):
                at = slice(i * width, (i + 1) * width)
                return w_hi[slot][:, at], w_lo[slot][:, at]

            def pair(hi, lo, k, at=slice(0, SEQ)):
                return hi[:, k, at], lo[:, k, at]

            def column_unit(ready, slot, bank, xg0=None, halfway=()):
                for k in range(KC):
                    if k in ready:
                        pe.wait_ge(*ready[k])
                    if xg0 is not None:
                        pe.wait_ge(xg_ready, xg0 + k + 1)
                    last = split_product(proj[bank][:, 0:SEQ], tile(slot, k), pair(xg_hi, xg_lo, k), k == 0, k == KC - 1)
                    if k == KC // 2 - 1:
                        for product in halfway:
                            product()
                last.then_inc(unit_done, 1)

            def small_bank(use):
                at = SMALL_AT[use]
                if at >= 2:
                    pe.wait_ge(small_read, at - 1)
                return small[at % 2]

            def sum_over_channels(n):
                bank = small_bank(("rms", n))
                pe.wait_ge(sumsq_step, sumsq_steps(n + 1))
                last = n == len(PHASES)
                i = nc.tensor.matmul(bank[:, 0:SEQ], ones[:], sumsq[:], start=True, stop=not last)
                if last:
                    pe.wait_ge(square_ready, SCALAR_SQUARES + 1)
                    i = nc.tensor.matmul(bank[:, 0:SEQ], ones[:], square[:], start=False, stop=True)
                i.then_inc(small_done, 1)

            def turn_mean(n):
                bank = small_bank(("mean_col", n))
                pe.wait_ge(small_read, SMALL_AT[("rms", n)] + 1)
                pe.wait_ge(tables_loaded, 16 * N_TABLES)
                for t in range(TT):
                    last = nc.tensor.matmul(bank[:, t:t + 1], mean_sq[:, P * t:P * t + P], ident[:, 0:1], start=True, stop=True)
                last.then_inc(small_done, 1)

            def token_unit(u, half, banks, xg0=None):
                pe.wait_ge(lo_ready, u + 1)
                for i in range(KC // 2):
                    k = KC // 2 * half + i
                    if xg0 is not None:
                        pe.wait_ge(xg_ready, xg0 + k + 1)
                    for t in range(TT):
                        last = split_product(proj[banks + t][:, 0:2 * P], pair(xg_hi, xg_lo, k, slice(P * t, P * t + P)),
                                             tile(u % SLOTS, i, 2 * P), k == 0, k == KC - 1)
                last.then_inc(unit_done, 1)

            first_units = [{0: (first_lo, 1), 2: (first_lo, 2), 4: (first_lo, 3), 6: (lo_ready, 1)},
                           {0: (first_lo, 4), 4: (lo_ready, 2)}]

            def ffn(n):
                u0, p0 = UNIT0[n], PROJ0[n]
                for u in range(SLOTS):
                    if p0:
                        pe.wait_ge(proj_read, p0 + u - 3)
                    ready = {0: (lo_ready, u0 + u + 1)}
                    if u0 + u < 2:
                        ready = first_units[u]
                    column_unit(ready, u, u, KC * n if u == 0 else None,
                                halfway=[partial(sum_over_channels, n)] if n and u == 1 else ())
                    if n == 0 and u == 1:
                        sum_over_channels(n)
                with pe.Fori(SLOTS, IN_UNITS[FFN], SLOTS) as u:
                    for s in range(SLOTS):
                        pe.wait_ge(proj_read, u + (p0 + s - 3))
                        column_unit({0: (lo_ready, u + (u0 + s + 1))}, s, s)

            def ffn_out(n):
                u0, c0 = UNIT0[n] + IN_UNITS[FFN], h0(n)

                def chunk(j, b, peeled):
                    first = peeled and b == 0
                    if n or not peeled:
                        pe.wait_ge(x_ready, j + (KC * n + b - 1))
                    for half in range(2):
                        slot = 2 * b + half
                        pe.wait_ge(lo_ready, j * 2 + (u0 + slot + 1))
                        for i in range(TILES_OUT):
                            c = TILES_OUT * half + i
                            if first and (c == 0 or c >= FC - 2):
                                pe.wait_ge(h_ready, c0 + (FC - 2 if c == 0 else c + 1))
                            last = split_product(down[b][:, 0:SEQ], tile(slot, i), pair(h_hi, h_lo, c), c == 0, c == FC - 1)
                        last.then_inc(unit_done, 1)

                for b in range(2):
                    chunk(0, b, True)
                with pe.Fori(2, KC, 2) as j:
                    for b in range(2):
                        chunk(j, b, False)

            def out_chunks(n, ks, js=(0, 1)):
                u0, c0 = UNIT0[n] + 12, h0(n)
                if PHASES[n] == MIX:
                    h_waits = [(small_read, SMALL_AT[("dft_pos", g)] + 1) for g in range(N_GROUPS)]
                    h_waits += [(h_ready, c0 + g + 1) for g in range(N_GROUPS)]
                else:
                    h_waits = [(small_read, SMALL_AT[("context", h)] + 1) for h in range(N_HEADS)]
                if 0 in ks:
                    pe.wait_ge(lo_ready, u0 + js[-1] + 1)
                    if PHASES[n] == ATT and js[-1] < 2:
                        pe.wait_ge(probs_t_ready, TURN_IN_DOWN)
                for k in ks:
                    pe.wait_ge(*h_waits[k])
                    for j in js:
                        last = split_product(out_bank(n, j)[:, 0:SEQ], tile((u0 + j) % SLOTS, k), pair(h_hi, h_lo, k), k == 0, k == KC - 1)
                        if k == KC - 1:
                            last.then_inc(unit_done, 1)

            def out_units(n, js):
                u0 = UNIT0[n] + 12
                for j in js:
                    pe.wait_ge(lo_ready, u0 + j + 1)
                    if bank_before(j) >= 0:
                        pe.wait_ge(x_ready, KC * n + bank_before(j) + 1)
                    for k in range(KC):
                        last = split_product(out_bank(n, j)[:, 0:SEQ], tile((u0 + j) % SLOTS, k), pair(h_hi, h_lo, k), k == 0, k == KC - 1)
                    last.then_inc(unit_done, 1)

            def mix(n):
                u0, p0 = UNIT0[n], PROJ0[n]

                def dft_ch(g):
                    bank = small_bank(("dft_ch", g))
                    pe.wait_ge(proj_read, p0 + 4 + g + 1)
                    for t in range(TT):
                        last = nc.tensor.matmul(bank[:, 2 * P * t:2 * P * t + 2 * P], f_in[:, g % 2, P * t:P * t + P], dft_c[:],
                                                start=True, stop=True)
                    last.then_inc(small_done, 1)

                def dft_pos(g):
                    bank = small_bank(("dft_pos", g))
                    pe.wait_ge(small_read, SMALL_AT[("dft_ch", g)] + 1)
                    pe.wait_ge(dft_lo_ready, 1)
                    for t in range(TT):
                        for part in range(2):
                            at = slice(2 * P * t + P * part, 2 * P * t + P * part + P)
                            last = split_product(bank[:, 0:SEQ], pair(f_ch_hi, f_ch_lo, g % 2, at),
                                                 (dft_p_hi[:, t, part, :], dft_p_lo[:, t, part, :]), t + part == 0, t + part == 2)
                    last.then_inc(small_done, 1)

                def spatial(g):
                    bank = small_bank(("spatial", g))
                    pe.wait_ge(v_norm_ready, 1)
                    for t in range(TT):
                        last = nc.tensor.matmul(bank[:, P * t:P * t + P], v_norm[:, t, P * g:P * g + P], w_s[:, g, :],
                                                start=True, stop=True)
                    last.then_inc(small_done, 1)

                for s in range(12):
                    if s < 4:
                        if s % 2 == 0:
                            pe.wait_ge(proj_read, p0 + s - 2)
                        token_unit(u0 + s, s % 2, s // 2 * 2, KC * n if s < 2 else None)
                    else:
                        pe.wait_ge(proj_read, p0 + s - 3)
                        column_unit({0: (lo_ready, u0 + s + 1)}, s % 4, s % 4)
                    if s == 0:
                        sum_over_channels(n)
                    if s == 1:
                        turn_mean(n)
                    if 6 <= s < 10:
                        dft_pos(s - 6)
                    if 5 <= s < 9:
                        dft_ch(s - 5)
                    for g in GATES_AT.get(s, ()):
                        spatial(g)
                out_chunks(n, range(KC))
                pe.wait_ge(proj_read, p0 + 12)
                out_chunks(n, range(KC), (2,))
                out_units(n, range(3, KC))

            def att(n):
                u0, p0 = UNIT0[n], PROJ0[n]

                def sum_key_squares(h):
                    bank = small_bank(("k_sum", h))
                    pe.wait_ge(head_copied, h + 1)
                    nc.tensor.matmul(bank[:, 0:SEQ], ones[:], head_sq[:, h, :], start=True, stop=True).then_inc(small_done, 1)

                def swap_key_pairs(h):
                    bank = small_bank(("k_swap", h))
                    pe.wait_ge(head_copied, h + 1)
                    pe.wait_ge(rope_ready, 4)
                    nc.tensor.matmul(bank[:, 0:SEQ], swap_k, head_raw[:, h, :], start=True, stop=True).then_inc(small_done, 1)

                def rotate(h):
                    i = N_KV + h
                    bank = small_bank(("rotate", h))
                    pe.wait_ge(head_copied, i + 1)
                    nc.tensor.matmul(bank[:, 0:SEQ], swap_q, head_raw[:, i % 2, :], start=True, stop=True)
                    for t in range(TT):
                        last = nc.tensor.matmul(bank[:, SEQ + t:SEQ + t + 1], head_sq[:, i % 2, P * t:P * t + P], ones[:, 0:1],
                                                start=True, stop=True)
                    last.then_inc(small_done, 1)

                def scores(h):
                    pe.wait_ge(rot_ready, N_KV + h + 1)
                    if h >= 2:
                        pe.wait_ge(probs_ready, h - 1)
                    else:
                        pe.wait_ge(proj_read, p0 + TT)
                    for t in range(TT):
                        last = nc.tensor.matmul(proj[2 + h % 2][:, SEQ * t:SEQ * t + SEQ], q_rot[:, h % 2, P * t:P * t + P],
                                                k_rot[:, h // (N_HEADS // N_KV), :], start=True, stop=True)
                    last.then_inc(scores_done, 1)

                def turn(h):
                    pe.wait_ge(probs_n_ready, h + 1)
                    if h >= 2:
                        pe.wait_ge(probs_t_ready, h - 1)
                    if h == TURN_IN_DOWN:
                        pe.wait_ge(head_copied, HEADS)
                    for kt in range(TT):
                        for t in range(TT):
                            at = SEQ * kt + P * t
                            last = nc.tensor.transpose(turn_bank(h)[:, at:at + P], probs_n[:, h % 2, t, P * kt:P * kt + P], ident)
                    last.then_inc(turned, 1)

                def context(h):
                    bank = small_bank(("context", h))
                    pe.wait_ge(probs_t_ready, h + 1)
                    kv = h // (N_HEADS // N_KV)
                    for kt in range(TT):
                        last = nc.tensor.matmul(bank[:, 0:SEQ], v_keys[:, kt, HEAD_DIM * kv:HEAD_DIM * kv + HEAD_DIM],
                                                probs_t[:, h % 2, kt, :], start=kt == 0, stop=kt == TT - 1)
                    last.then_inc(small_done, 1)

                for s in range(12):
                    for h in head_in_step(s, SCORE):
                        scores(h)
                    if s < 2:
                        column_unit({0: (lo_ready, u0 + s + 1)}, s, s, KC * n if s == 0 else None)
                    elif s < 4:
                        token_unit(u0 + s, s - 2, 2)
                    else:
                        if s > 4:
                            pe.wait_ge(head_copied, s - 3)
                        column_unit({0: (lo_ready, u0 + s + 1)}, s % 4, s % 2, halfway=[partial(rotate, h) for h in head_in_step(s, ROTATE)])
                    if s == 0:
                        sum_over_channels(n)
                    if s == 1:
                        turn_mean(n)
                        sum_key_squares(0)
                    if s == 2:
                        swap_key_pairs(0)
                        sum_key_squares(1)
                    if s == 3:
                        swap_key_pairs(1)
                    for h in head_in_step(s, CONTEXT):
                        context(h)
                    for h in head_in_step(s, SCORE):
                        turn(h)
                scores(6)
                out_chunks(n, (0,))
                rotate(7)
                out_chunks(n, (1, 2))
                scores(7)
                context(5)
                turn(6)
                out_chunks(n, (3, 4))
                context(6)
                turn(7)
                out_chunks(n, (5,))
                pe.wait_ge(probs_ready, 7)
                out_chunks(n, range(2), (2,))
                context(7)
                out_chunks(n, (6,))
                out_chunks(n, range(2, 7), (2,))
                out_chunks(n, (7,), (0, 1, 2))
                pe.wait_ge(probs_ready, 8)
                out_units(n, range(3, KC))

            pe.wait_ge(ones_ready, 1)
            for _ in range(WARM_UP):
                nc.tensor.matmul(proj[3][:, 0:P], ones[:], ones[:], start=True, stop=True)
            for n, kind in enumerate(PHASES):
                if kind == FFN:
                    ffn(n)
                    ffn_out(n)
                else:
                    {MIX: mix, ATT: att}[kind](n)
            sum_over_channels(len(PHASES))


def tiles(w, k, columns):
    return w.reshape(k, P, -1, columns).transpose(2, 1, 0, 3).reshape(-1, P, k * columns)


def ffn_in_units(gate, up):
    both = np.stack([tiles(gate, KC, P), tiles(up, KC, P)], axis=1)
    return both.reshape(2 * FC, P, TILES_IN * P)


def ffn_out_units(w):
    halves = w.reshape(2, TILES_OUT, P, KC, P).transpose(3, 0, 2, 1, 4)
    return halves.reshape(2 * KC, P, TILES_OUT * P)


def token_units(w):
    return w.reshape(2, KC // 2, P, -1, 2 * P).transpose(3, 0, 2, 1, 4).reshape(-1, P, TILES_IN * P)


def dft_tables():
    c = 2 * np.pi * np.outer(np.arange(P), np.arange(P)) / P
    channels = np.concatenate([np.cos(c), np.sin(c)], axis=1) / np.sqrt(P)
    t = 2 * np.pi * np.outer(np.arange(SEQ), np.arange(SEQ)) / SEQ
    positions = np.stack([np.cos(t), -np.sin(t)], axis=1) / np.sqrt(SEQ)
    positions = positions.reshape(TT, P, 2, SEQ).transpose(1, 0, 2, 3)
    return channels.astype(np.float32), np.ascontiguousarray(positions.astype(np.float32))


def rope_table():
    per_axis = HEAD_DIM // 4
    freq = 10000.0 ** (-np.arange(per_axis) / per_axis)
    t = np.arange(SEQ)
    angle = np.concatenate([np.outer(freq, t // GRID_W), np.outer(freq, t % GRID_W)])
    cos, sin = np.repeat(np.cos(angle), 2, axis=0), np.repeat(np.sin(angle), 2, axis=0)
    sin[0::2] *= -1
    return np.ascontiguousarray(np.stack([cos, sin], axis=1).astype(np.float32))


def kernel(**inputs):
    import concourse.bacc as bacc
    from concourse.bass_utils import run_bass_kernel_spmd

    a = {name: np.asarray(value) for name, value in inputs.items()}
    ffns = [(a[f + "_w_gate"][layer], a[f + "_w_up"][layer], a[f + "_w_down"][layer])
            for layer in range(2) for f in ("ffn1", "ffn2")]
    w_in, w_qkv = a["ab_w_in"][0], a["attn_w_qkv"][0]
    f_end, u_end = N_GROUPS * P, 2 * N_GROUPS * P
    q_end, k_end = N_HEADS * HEAD_DIM, (N_HEADS + N_KV) * HEAD_DIM
    norms = [a[name][layer] for layer in range(2) for name in ("ffn1_norm", "mix_norm", "ffn2_norm")] + [a["final_norm"]]
    dft_channels, dft_positions = dft_tables()
    swap = np.eye(P, dtype=np.float32)[np.arange(P) ^ 1]
    arrays = {
        "x_t": a["x"][0].T.reshape(KC, P, SEQ).transpose(1, 0, 2),
        "ffn_in_w": np.concatenate([ffn_in_units(gate, up) for gate, up, _ in ffns]),
        "ffn_out_w": np.concatenate([ffn_out_units(down) for _, _, down in ffns]),
        "mix_w": np.concatenate([token_units(w_in[:, u_end:]), tiles(w_in[:, :f_end], KC, P),
                                 tiles(w_in[:, f_end:u_end], KC, P), tiles(a["ab_w_out"][0], KC, P)]),
        "attn_w": np.concatenate([tiles(w_qkv[:, q_end:k_end], KC, P), token_units(w_qkv[:, k_end:]),
                                  tiles(w_qkv[:, :q_end], KC, P), tiles(a["attn_w_o"][0], KC, P)]),
        "gains": np.stack([g.reshape(KC, P).T for g in norms], axis=1),
        "head_gains": np.stack([*a["ab_v_norm"][0], a["attn_q_norm"][0], a["attn_k_norm"][0]], axis=1),
        "spatial_w": a["ab_w_s"][0].transpose(2, 0, 1),
        "spatial_b": np.broadcast_to(a["ab_b_s"][0][None, :, None, :], (P, N_GROUPS, TT, P)),
        "dft_channels": dft_channels,
        "dft_positions": dft_positions,
        "rope": rope_table(),
        "matrices": np.stack([np.eye(P, dtype=np.float32), swap], axis=1),
    }
    arrays = {name: np.ascontiguousarray(value) for name, value in arrays.items()}
    nc = bacc.Bacc("TRN2", target_bir_lowering=False, num_devices=1)
    aps = {name: nc.dram_tensor(name, value.shape, F32, kind="ExternalInput").ap() for name, value in arrays.items()}
    out = nc.dram_tensor("out_t", (P, KC, SEQ), F32, kind="ExternalOutput").ap()
    trunk_program(nc, out=out, **aps)
    result = run_bass_kernel_spmd(nc, [arrays], core_ids=[0])
    y = result.results[0]["out_t"]
    return y.transpose(1, 0, 2).reshape(1, D_MODEL, SEQ).transpose(0, 2, 1)
```
